# Optimizing a Trainium2 kernel written in Bass

```python
import jax, jax.numpy as jnp
from jax import lax
import numpy as np

D_MODEL = 1024
BATCH = 1
SEQ = 256
DEPTH = 2

GRID_W = 64
CTX_LEN = 256
W_CONV = D_MODEL
W_LRU = D_MODEL
W_EVEN = W_CONV + W_LRU
N_LRU_HEADS = 8
LRU_HEAD_DIM = W_LRU // N_LRU_HEADS
CONV_WIDTH = 31
CONV_PAD = (15, 15)
SHORT_CONV_WIDTH = 4
SHORT_CONV_PAD = (2, 1)
LRU_C = 8.0
W_POOL = 2 * D_MODEL
POOL_WINDOWS = (2, 4, 8, 16)
N_POOL_GROUPS = len(POOL_WINDOWS)
POOL_GROUP_DIM = W_POOL // N_POOL_GROUPS
N_EVEN = (DEPTH + 1) // 2
N_ODD = DEPTH // 2
RMS_EPS = 1e-6
LN_EPS = 1e-5


def rmsnorm(x, g):
    xf = x.astype(jnp.float32)
    y = xf * lax.rsqrt(jnp.mean(xf * xf, axis=-1, keepdims=True) + RMS_EPS)
    return (y * g.astype(jnp.float32)).astype(x.dtype)

def layernorm(x, g, b):
    xf = x.astype(jnp.float32)
    mu = jnp.mean(xf, axis=-1, keepdims=True)
    var = jnp.mean(jnp.square(xf - mu), axis=-1, keepdims=True)
    y = (xf - mu) * lax.rsqrt(var + LN_EPS) * g.astype(jnp.float32) + b.astype(jnp.float32)
    return y.astype(x.dtype)

def modulate(h, shift, scale):
    return h * (1 + scale) + shift

def depthwise_conv(u, w, b, pad):
    y = lax.conv_general_dilated(
        u, w[:, None, :].astype(u.dtype), window_strides=(1,), padding=(pad,),
        dimension_numbers=("NWC", "WIO", "NWC"), feature_group_count=u.shape[-1])
    return y + b.astype(u.dtype)

def conformer_conv(va, vg, p):
    u = va * jax.nn.sigmoid(vg)
    u = depthwise_conv(u, p["conv_w"], p["conv_b"], CONV_PAD)
    return jax.nn.silu(layernorm(u, p["ln_g"], p["ln_b"]))

def lru_coeffs(u2, p):
    bn, n = u2.shape[0], u2.shape[1]
    uf = u2.astype(jnp.float32)
    uh = uf.reshape(bn, n, 2, N_LRU_HEADS, LRU_HEAD_DIM)
    gr = jnp.einsum("bnkhi,khij->bnkhj", uh, p["w_r"].astype(jnp.float32)).reshape(bn, n, 2, W_LRU)
    gi = jnp.einsum("bnkhi,khij->bnkhj", uh, p["w_i"].astype(jnp.float32)).reshape(bn, n, 2, W_LRU)
    r = jax.nn.sigmoid(gr + p["b_r"].astype(jnp.float32))
    i = jax.nn.sigmoid(gi + p["b_i"].astype(jnp.float32))
    log_a = -LRU_C * r * jax.nn.softplus(-p["lam"].astype(jnp.float32))
    a = jnp.exp(log_a)
    bx = jnp.sqrt(-jnp.expm1(2.0 * log_a)) * (i * uf)
    return a, bx

def lru_scan(a, bx, h0, with_outputs):
    def step(h, ab):
        at, bt = ab
        h = at * h + bt
        return h, (h if with_outputs else None)
    hT, hs = lax.scan(step, h0, (jnp.swapaxes(a, 0, 1), jnp.swapaxes(bx, 0, 1)))
    return hT, hs

def rglru_branch(xb, p, h0, with_outputs):
    u = depthwise_conv(xb, p["sconv_w"], p["sconv_b"], SHORT_CONV_PAD)
    u2 = jnp.stack([u, u[:, ::-1]], axis=2)
    a, bx = lru_coeffs(u2, p)
    hT, hs = lru_scan(a, bx, h0, with_outputs)
    if not with_outputs:
        return None, hT
    y = hs[:, :, 0] + hs[::-1, :, 1]
    return jnp.swapaxes(y, 0, 1).astype(xb.dtype), hT

def even_mixer(h, h0, p):
    z = h @ p["w_in"]
    va, vg, ga, xb, gb = jnp.split(
        z, [W_CONV, 2 * W_CONV, 3 * W_CONV, 3 * W_CONV + W_LRU], axis=-1)
    y_a = conformer_conv(va, vg, p) * jax.nn.silu(ga)
    y_b, hT = rglru_branch(xb, p, h0, True)
    y_b = y_b * jax.nn.silu(gb)
    return jnp.concatenate([y_a, y_b], axis=-1) @ p["w_out"], hT

def multiscale_pool(u):
    n = u.shape[1]
    uf = u.astype(jnp.float32)
    s = jnp.pad(jnp.cumsum(uf, axis=1), ((0, 0), (1, 0), (0, 0)))
    t = jnp.arange(n)
    parts = []
    for g, w in enumerate(POOL_WINDOWS):
        lo = jnp.clip(t - w // 2, 0, n)
        hi = jnp.clip(t + w // 2, 0, n)
        sg = s[:, :, g * POOL_GROUP_DIM:(g + 1) * POOL_GROUP_DIM]
        cnt = (hi - lo).astype(jnp.float32)[None, :, None]
        parts.append((sg[:, hi] - sg[:, lo]) / cnt)
    return (jnp.concatenate(parts, axis=-1) - uf).astype(u.dtype)

def odd_mixer(h, p, on_grid):
    bn, n = h.shape[0], h.shape[1]
    z = h @ p["w_in"]
    u, g = jnp.split(z, [W_POOL], axis=-1)
    if on_grid:
        rows = n // GRID_W
        d = multiscale_pool(u.reshape(bn * rows, GRID_W, W_POOL)).reshape(bn, n, W_POOL)
    else:
        d = multiscale_pool(u)
    d = d.reshape(bn, n, N_POOL_GROUPS, POOL_GROUP_DIM)
    y = jnp.einsum("bngi,gij->bngj", d, p["w_grp"]).reshape(bn, n, W_POOL) * p["scale"]
    return (y * jax.nn.silu(g)) @ p["w_out"]

def first_inputs(seed: int = 0) -> dict:
    key = jax.random.key(seed)
    ks = jax.random.split(key, 32)
    f32 = jnp.float32

    def nrm(k, shape, s):
        return s * jax.random.normal(k, shape, f32)

    ua = jax.random.uniform(ks[20], (N_EVEN, 2, W_LRU), f32, 0.9, 0.999)
    pa = ua ** (1.0 / LRU_C)
    lam = jnp.log(pa) - jnp.log1p(-pa)
    return {
        "x": nrm(ks[0], (BATCH, SEQ, D_MODEL), 1.0),
        "c": nrm(ks[1], (BATCH, D_MODEL), 1.0),
        "ctx": nrm(ks[2], (BATCH, CTX_LEN, D_MODEL), 1.0),
        "c_ctx": nrm(ks[3], (D_MODEL,), 1.0),
        "norm_g": 1.0 + nrm(ks[4], (DEPTH, D_MODEL), 0.1),
        "mod_w": nrm(ks[5], (DEPTH, D_MODEL, 3 * D_MODEL), 0.5 * D_MODEL ** -0.5),
        "mod_b": nrm(ks[6], (DEPTH, 3 * D_MODEL), 0.02),
        "ev_w_in": nrm(ks[7], (N_EVEN, D_MODEL, 3 * W_CONV + 2 * W_LRU), D_MODEL ** -0.5),
        "ev_conv_w": nrm(ks[8], (N_EVEN, CONV_WIDTH, W_CONV), CONV_WIDTH ** -0.5),
        "ev_conv_b": nrm(ks[9], (N_EVEN, W_CONV), 0.02),
        "ev_ln_g": 1.0 + nrm(ks[10], (N_EVEN, W_CONV), 0.1),
        "ev_ln_b": nrm(ks[11], (N_EVEN, W_CONV), 0.02),
        "ev_sconv_w": nrm(ks[12], (N_EVEN, SHORT_CONV_WIDTH, W_LRU), SHORT_CONV_WIDTH ** -0.5),
        "ev_sconv_b": nrm(ks[13], (N_EVEN, W_LRU), 0.02),
        "ev_w_r": nrm(ks[14], (N_EVEN, 2, N_LRU_HEADS, LRU_HEAD_DIM, LRU_HEAD_DIM), LRU_HEAD_DIM ** -0.5),
        "ev_b_r": nrm(ks[15], (N_EVEN, 2, W_LRU), 0.02),
        "ev_w_i": nrm(ks[16], (N_EVEN, 2, N_LRU_HEADS, LRU_HEAD_DIM, LRU_HEAD_DIM), LRU_HEAD_DIM ** -0.5),
        "ev_b_i": nrm(ks[17], (N_EVEN, 2, W_LRU), 0.02),
        "ev_lam": lam,
        "ev_w_out": nrm(ks[18], (N_EVEN, W_EVEN, D_MODEL), W_EVEN ** -0.5),
        "od_w_in": nrm(ks[21], (N_ODD, D_MODEL, 2 * W_POOL), D_MODEL ** -0.5),
        "od_w_grp": nrm(ks[22], (N_ODD, N_POOL_GROUPS, POOL_GROUP_DIM, POOL_GROUP_DIM), POOL_GROUP_DIM ** -0.5),
        "od_scale": 1.0 + nrm(ks[23], (N_ODD, W_POOL), 0.1),
        "od_w_out": nrm(ks[24], (N_ODD, W_POOL, D_MODEL), W_POOL ** -0.5),
        "final_g": 1.0 + nrm(ks[25], (D_MODEL,), 0.1),
    }

def first_block(x, c, ctx, c_ctx, norm_g, mod_w, mod_b,
              ev_w_in, ev_conv_w, ev_conv_b, ev_ln_g, ev_ln_b, ev_sconv_w, ev_sconv_b,
              ev_w_r, ev_b_r, ev_w_i, ev_b_i, ev_lam, ev_w_out,
              od_w_in, od_w_grp, od_scale, od_w_out, final_g):
    bn = x.shape[0]
    sc = jax.nn.silu(c)
    scc = jax.nn.silu(c_ctx)
    for l in range(DEPTH):
        ctx_out_needed = any(j % 2 == 0 for j in range(l + 1, DEPTH))
        shift, scale, gate = jnp.split(sc @ mod_w[l] + mod_b[l], 3, axis=-1)
        hx = modulate(rmsnorm(x, norm_g[l]), shift[:, None], scale[:, None])
        if ctx_out_needed or l % 2 == 0:
            shift_c, scale_c, gate_c = jnp.split(scc @ mod_w[l] + mod_b[l], 3, axis=-1)
            hc = modulate(rmsnorm(ctx, norm_g[l]), shift_c, scale_c)
        j = l // 2
        if l % 2 == 0:
            pe = {"w_in": ev_w_in[j], "conv_w": ev_conv_w[j], "conv_b": ev_conv_b[j],
                  "ln_g": ev_ln_g[j], "ln_b": ev_ln_b[j], "sconv_w": ev_sconv_w[j],
                  "sconv_b": ev_sconv_b[j], "w_r": ev_w_r[j], "b_r": ev_b_r[j],
                  "w_i": ev_w_i[j], "b_i": ev_b_i[j], "lam": ev_lam[j], "w_out": ev_w_out[j]}
            h0 = jnp.zeros((bn, 2, W_LRU), jnp.float32)
            if ctx_out_needed:
                out_c, h_ctx = even_mixer(hc, h0, pe)
            else:
                xb_c = hc @ pe["w_in"][:, 3 * W_CONV:3 * W_CONV + W_LRU]
                _, h_ctx = rglru_branch(xb_c, pe, h0, False)
            out_x, _ = even_mixer(hx, h_ctx, pe)
        else:
            po = {"w_in": od_w_in[j], "w_grp": od_w_grp[j], "scale": od_scale[j], "w_out": od_w_out[j]}
            if ctx_out_needed:
                out_c = odd_mixer(hc, po, False)
            out_x = odd_mixer(hx, po, True)
        x = x + gate[:, None] * out_x
        if ctx_out_needed:
            ctx = ctx + gate_c * out_c
    return rmsnorm(x, final_g)


DEPTH_2 = 1


A_HEADS = 4
A_DK = 128
A_DV = 128
A_KW = A_HEADS * A_DK
A_VW = A_HEADS * A_DV
A_CHUNK = 64

B_GROUPS = 4
B_GW = 128
B_W = B_GROUPS * B_GW
B_CHUNK = 2 * GRID_W

D_FF = -(-8 * D_MODEL // (3 * 256)) * 256

N_MOD = 6
EPS = 1e-6

CTX_STATE_COLS = 2 * A_KW + A_VW
SPLIT_IDX = (A_KW, 2 * A_KW, 2 * A_KW + A_VW, 3 * A_KW + A_VW, 3 * A_KW + 2 * A_VW,
             3 * A_KW + 2 * A_VW + B_W, 3 * A_KW + 2 * A_VW + 2 * B_W,
             3 * A_KW + 2 * A_VW + 2 * B_W + D_MODEL)
IN_COLS = 3 * A_KW + 2 * A_VW + 2 * B_W + 2 * D_MODEL


def rmsnorm_2(x, g):
    xf = x.astype(jnp.float32)
    y = xf * lax.rsqrt(jnp.mean(xf * xf, axis=-1, keepdims=True) + EPS)
    return (y * g.astype(jnp.float32)).astype(x.dtype)

def layernorm_2(x, g, b):
    xf = x.astype(jnp.float32)
    mu = jnp.mean(xf, axis=-1, keepdims=True)
    var = jnp.mean(jnp.square(xf - mu), axis=-1, keepdims=True)
    y = (xf - mu) * lax.rsqrt(var + EPS) * g.astype(jnp.float32) + b.astype(jnp.float32)
    return y.astype(x.dtype)

def modulate_2(h, shift, scale):
    return h * (1 + scale) + shift

def split_heads(t):
    return t.reshape(t.shape[0], t.shape[1], A_HEADS, -1).astype(jnp.float32)

def flip_seq(t):
    return jnp.flip(t, axis=1)

def forget_gate(f_logit, lb):
    f = lb + (1 - lb) * jax.nn.sigmoid(f_logit.astype(jnp.float32))
    return jnp.log(f), 1 - f

def hgrn2_chunked(q, k, logf, v, s0):
    b_, L = q.shape[:2]
    n = L // A_CHUNK
    rs = lambda t: t.reshape(b_, n, A_CHUNK, *t.shape[2:])
    q, k, logf, v = rs(q), rs(k), rs(logf), rs(v)
    bcum = jnp.cumsum(logf, axis=2)
    blast = bcum[:, :, -1:]
    mid = 0.5 * blast
    q_in = q * jnp.exp(bcum - mid)
    k_in = k * jnp.exp(mid - bcum)
    scores = jnp.einsum('bnthd,bnshd->bnhts', q_in, k_in)
    mask = jnp.tril(jnp.ones((A_CHUNK, A_CHUNK), dtype=bool))
    scores = jnp.where(mask, scores, 0.0)
    o_intra = jnp.einsum('bnhts,bnshe->bnthe', scores, v)
    d_state = jnp.einsum('bnshd,bnshe->bnhde', k * jnp.exp(blast - bcum), v)
    decay = jnp.exp(blast[:, :, 0])

    def step(s, inp):
        a, d = inp
        return a[..., None] * s + d, s

    s_final, s_in = lax.scan(step, s0, (jnp.moveaxis(decay, 1, 0), jnp.moveaxis(d_state, 1, 0)))
    s_in = jnp.moveaxis(s_in, 0, 1)
    o_inter = jnp.einsum('bnthd,bnhde->bnthe', q * jnp.exp(bcum), s_in)
    o = (o_intra + o_inter).reshape(b_, L, A_HEADS, A_DV)
    return o, s_final

def hgrn2_final_state(k, logf, v):
    bcum = jnp.cumsum(logf, axis=1)
    w = k * jnp.exp(bcum[:, -1:] - bcum)
    return jnp.einsum('blhd,blhe->bhde', w, v)

def chunk_sgu(u, v, ln_g, ln_b, w_s, b_s, n_chunks):
    b_, L = u.shape[:2]
    v = layernorm_2(v, ln_g, ln_b)
    vc = v.reshape(b_, n_chunks, B_CHUNK, B_GROUPS, B_GW)
    mixed = jnp.einsum('gts,bnsgc->bntgc', w_s, vc) + jnp.transpose(b_s)[:, :, None]
    return u * mixed.reshape(b_, L, B_W)

def token_mixers(p, lb, g_norm_a, ln_v_g, ln_v_b, w_s, b_s, w_pa, w_pb, w_o, s0_f, s0_b, n_chunks_b):
    f_f, f_b, i_in, q, og, u, v, ga, gb = jnp.split(p, SPLIT_IDX, axis=-1)
    b_, L = p.shape[:2]
    logf_f, k_f = forget_gate(f_f, lb[0])
    logf_b, k_b = forget_gate(f_b, lb[1])
    qh, vh = split_heads(q), split_heads(i_in)
    o_f, s_f = hgrn2_chunked(qh, split_heads(k_f), split_heads(logf_f), vh, s0_f)
    o_b, s_b = hgrn2_chunked(flip_seq(qh), flip_seq(split_heads(k_b)), flip_seq(split_heads(logf_b)),
                             flip_seq(vh), s0_b)
    o_a = rmsnorm_2(o_f + flip_seq(o_b), g_norm_a).reshape(b_, L, A_VW).astype(p.dtype)
    o_a = o_a * jax.nn.silu(og)
    o_b_mlp = chunk_sgu(jax.nn.gelu(u), jax.nn.gelu(v), ln_v_g, ln_v_b, w_s, b_s, n_chunks_b)
    merged = jax.nn.sigmoid(ga) * (o_a @ w_pa) + jax.nn.sigmoid(gb) * (o_b_mlp @ w_pb)
    return merged @ w_o, s_f, s_b

def swiglu(h, w_up, w_down):
    a, b = jnp.split(h @ w_up, 2, axis=-1)
    return (jax.nn.silu(a) * b) @ w_down

def second_inputs(seed: int = 0) -> dict:
    key = jax.random.key(seed)
    ks = jax.random.split(key, 21)
    nrm = lambda k, shape, s: jax.random.normal(k, shape, jnp.float32) * s
    return {
        'x': nrm(ks[0], (BATCH, SEQ, D_MODEL), 1.0),
        'c': nrm(ks[1], (BATCH, D_MODEL), 1.0),
        'ctx': nrm(ks[2], (BATCH, CTX_LEN, D_MODEL), 1.0),
        'c_ctx': nrm(ks[3], (D_MODEL,), 1.0),
        'w_mod': nrm(ks[4], (DEPTH_2, D_MODEL, N_MOD * D_MODEL), 0.5 * D_MODEL ** -0.5),
        'b_mod': nrm(ks[5], (DEPTH_2, N_MOD * D_MODEL), 0.01),
        'g_mix': 1.0 + nrm(ks[6], (DEPTH_2, D_MODEL), 0.1),
        'g_ffn': 1.0 + nrm(ks[7], (DEPTH_2, D_MODEL), 0.1),
        'w_in': nrm(ks[8], (DEPTH_2, D_MODEL, IN_COLS), D_MODEL ** -0.5),
        'lb_gamma': nrm(ks[9], (DEPTH_2 + 1, 2, A_KW), 0.5),
        'g_norm_a': 1.0 + nrm(ks[10], (DEPTH_2, A_DV), 0.1),
        'ln_v_g': 1.0 + nrm(ks[11], (DEPTH_2, B_W), 0.1),
        'ln_v_b': nrm(ks[12], (DEPTH_2, B_W), 0.02),
        'w_s': nrm(ks[13], (DEPTH_2, B_GROUPS, B_CHUNK, B_CHUNK), 0.5 * B_CHUNK ** -0.5),
        'b_s': 1.0 + nrm(ks[14], (DEPTH_2, B_GROUPS, B_CHUNK), 0.1),
        'w_pa': nrm(ks[15], (DEPTH_2, A_VW, D_MODEL), A_VW ** -0.5),
        'w_pb': nrm(ks[16], (DEPTH_2, B_W, D_MODEL), B_W ** -0.5),
        'w_o': nrm(ks[17], (DEPTH_2, D_MODEL, D_MODEL), D_MODEL ** -0.5),
        'w_up': nrm(ks[18], (DEPTH_2, D_MODEL, 2 * D_FF), D_MODEL ** -0.5),
        'w_down': nrm(ks[19], (DEPTH_2, D_FF, D_MODEL), D_FF ** -0.5),
        'g_final': 1.0 + nrm(ks[20], (D_MODEL,), 0.1),
    }

def second_block(x, c, ctx, c_ctx, w_mod, b_mod, g_mix, g_ffn, w_in, lb_gamma, g_norm_a,
              ln_v_g, ln_v_b, w_s, b_s, w_pa, w_pb, w_o, w_up, w_down, g_final):
    bsz, L = x.shape[0], x.shape[1]
    rows = L // GRID_W
    n_chunks_lat = rows // 2
    n_chunks_ctx = ctx.shape[1] // B_CHUNK
    lb_all = jnp.cumsum(jax.nn.softmax(lb_gamma.astype(jnp.float32), axis=0), axis=0)
    for l in range(DEPTH_2):
        last = l == DEPTH_2 - 1
        lb = lb_all[l]
        mod = (jax.nn.silu(c) @ w_mod[l] + b_mod[l]).reshape(bsz, N_MOD, D_MODEL)
        mc = (jax.nn.silu(c_ctx) @ w_mod[l] + b_mod[l]).reshape(N_MOD, D_MODEL)
        hc = modulate_2(rmsnorm_2(ctx, g_mix[l]), mc[0], mc[1])
        if last:
            pc = hc @ w_in[l][:, :CTX_STATE_COLS]
            f_f, f_b, i_c = jnp.split(pc, (A_KW, 2 * A_KW), axis=-1)
            logf_f, k_f = forget_gate(f_f, lb[0])
            logf_b, k_b = forget_gate(f_b, lb[1])
            vh = split_heads(i_c)
            s_ctx_f = hgrn2_final_state(split_heads(k_f), split_heads(logf_f), vh)
            s_ctx_b = hgrn2_final_state(flip_seq(split_heads(k_b)), flip_seq(split_heads(logf_b)), flip_seq(vh))
        else:
            zeros = jnp.zeros((bsz, A_HEADS, A_DK, A_DV), jnp.float32)
            mix_c, s_ctx_f, s_ctx_b = token_mixers(hc @ w_in[l], lb, g_norm_a[l], ln_v_g[l], ln_v_b[l],
                                                   w_s[l], b_s[l], w_pa[l], w_pb[l], w_o[l],
                                                   zeros, zeros, n_chunks_ctx)
            ctx = ctx + mc[2] * mix_c
            hc2 = modulate_2(rmsnorm_2(ctx, g_ffn[l]), mc[3], mc[4])
            ctx = ctx + mc[5] * swiglu(hc2, w_up[l], w_down[l])
        h = modulate_2(rmsnorm_2(x, g_mix[l]), mod[:, 0, None], mod[:, 1, None])
        mix_x, _, _ = token_mixers(h @ w_in[l], lb, g_norm_a[l], ln_v_g[l], ln_v_b[l],
                                   w_s[l], b_s[l], w_pa[l], w_pb[l], w_o[l],
                                   s_ctx_f, s_ctx_b, n_chunks_lat)
        x = x + mod[:, 2, None] * mix_x
        h2 = modulate_2(rmsnorm_2(x, g_ffn[l]), mod[:, 3, None], mod[:, 4, None])
        x = x + mod[:, 5, None] * swiglu(h2, w_up[l], w_down[l])
    return rmsnorm_2(x, g_final)


def setup_inputs(seed=0):
    out = dict(first_inputs(seed))
    for name, value in second_inputs(seed + 1).items():
        if name != "x":
            out[name + "_2"] = value
    return out


def reference(
    x, c, ctx, c_ctx, norm_g, mod_w, mod_b, ev_w_in, ev_conv_w, ev_conv_b, ev_ln_g, ev_ln_b,
    ev_sconv_w, ev_sconv_b, ev_w_r, ev_b_r, ev_w_i, ev_b_i, ev_lam, ev_w_out, od_w_in, od_w_grp,
    od_scale, od_w_out, final_g, c_2, ctx_2, c_ctx_2, w_mod_2, b_mod_2, g_mix_2, g_ffn_2,
    w_in_2, lb_gamma_2, g_norm_a_2, ln_v_g_2, ln_v_b_2, w_s_2, b_s_2, w_pa_2, w_pb_2, w_o_2,
    w_up_2, w_down_2, g_final_2,
):
    x = first_block(
        x, c, ctx, c_ctx, norm_g, mod_w, mod_b, ev_w_in, ev_conv_w, ev_conv_b, ev_ln_g, ev_ln_b,
        ev_sconv_w, ev_sconv_b, ev_w_r, ev_b_r, ev_w_i, ev_b_i, ev_lam, ev_w_out, od_w_in,
        od_w_grp, od_scale, od_w_out, final_g,
    )
    return second_block(
        x, c_2, ctx_2, c_ctx_2, w_mod_2, b_mod_2, g_mix_2, g_ffn_2, w_in_2, lb_gamma_2,
        g_norm_a_2, ln_v_g_2, ln_v_b_2, w_s_2, b_s_2, w_pa_2, w_pb_2, w_o_2, w_up_2, w_down_2,
        g_final_2,
    )


_drawn_inputs = setup_inputs


def setup_inputs(seed=0):
    import zlib

    import numpy as np

    out = dict(_drawn_inputs(seed))
    spreads = {}
    factors = {'ev_conv_b': 8.0,
     'ev_ln_g': 5.793,
     'ev_ln_b': 21.59,
     'ev_b_r': 40.606,
     'ev_b_i': 21.451,
     'od_scale': 3.235,
     'ctx_2': 7.93,
     'c_ctx_2': 8.0,
     'b_mod_2': 5.358,
     'g_norm_a_2': 5.222,
     'ln_v_g_2': 8.0,
     'ln_v_b_2': 60.59,
     'b_s_2': 4.482}
    for name, (base, spread) in spreads.items():
        noise = np.random.default_rng([zlib.crc32(name.encode()), seed]).standard_normal(out[name].shape)
        drawn = base * np.exp(spread * noise) if base else spread * noise
        out[name] = __import__('jax').numpy.asarray(drawn.astype(out[name].dtype))
    for name, factor in factors.items():
        out[name] = (out[name] * factor).astype(out[name].dtype)
    return out
```

```python
from contextlib import ExitStack

import numpy as np
import concourse.bass as bass
from concourse import mybir

F32 = mybir.dt.float32
F32R = mybir.dt.float32r
I32 = mybir.dt.int32
ALU = mybir.AluOpType
ACT = mybir.ActivationFunctionType

P = 128
D = 1024
T = 256
KT = D // P
SLOTS = 4
HALF = 8 * P
EPS6, EPS5 = 1e-6, 1e-5
EPS = 1e-6
GRID_W = 64
CONV_TAPS = 31
CONV_LEFT = CONV_TAPS // 2
SCONV_TAPS = 4
SCONV_LEFT = 2
WINDOWS = (2, 4, 8, 16)
HEADS = 4
CHUNK = 64
CHUNKS = T // CHUNK
FF = 2816
FT = FF // P

PHASES = [
    ("xb", 2), ("vavg", 4), ("ga", 2), ("gb", 2), ("gates", 1), ("ya", 2), ("yb", 2),
    ("od_u", 4), ("od_g", 4), ("grp", 2), ("oda", 2), ("odb", 2),
    ("f", 2), ("i", 1), ("q", 1), ("uvo", 3), ("ga2", 2), ("gb2", 2), ("pab", 2), ("wo", 2), ("up", 11),
    ("dna", 2), ("dnb", 2), ("dnc", 2),
]
BASE, ROUNDS_OF = {}, {}
_n = 0
for _name, _rounds in PHASES:
    BASE[_name], ROUNDS_OF[_name] = _n, _rounds
    _n += _rounds
ROUNDS = _n
MOD0_ROUNDS = 4

MOD_TILES = KT + 3 * KT + 6 * KT
MOD_SLOTS = 4

PARAMS = [
    ("norm_g", 16), ("mod_b", 48), ("ev_conv_w", 31 * 8), ("ev_conv_b", 8), ("ev_ln_g", 8), ("ev_ln_b", 8),
    ("ev_sconv_w", 32), ("ev_sconv_b", 8), ("ev_b_r", 16), ("ev_b_i", 16), ("ev_lam", 16), ("od_scale", 16),
    ("final_g", 8), ("b_mod_2", 48), ("g_mix_2", 8), ("g_ffn_2", 8), ("lb_gamma_2", 16), ("g_norm_a_2", 1),
    ("ln_v_g_2", 4), ("ln_v_b_2", 4), ("g_final_2", 8),
]
COL = {}
_n = 0
for _name, _cols in PARAMS:
    COL[_name] = _n
    _n += _cols
NCOLS = _n

CONSTS = [("ident", P), ("ones", T), ("restart_f", T), ("restart_b", T), ("inv_count", len(WINDOWS) * GRID_W)]
CON = {}
_n = 0
for _name, _cols in CONSTS:
    CON[_name] = _n
    _n += _cols
NCONS = _n


class Steps:

    def __init__(self, eng, sem):
        self.eng, self.sem, self.n = eng, sem, 0

    def do(self, ins):
        ins.then_inc(self.sem, 1)
        self.n = self.n + 1
        return self.n

    def sync(self, n=None):
        self.eng.wait_ge(self.sem, self.n if n is None else n)

    def loop(self, count, per_round):
        start = self.n
        with self.eng.Fori(0, count) as i:
            self.n = i * per_round + start
            yield i
        self.n = start + count * per_round


def build(nc, ins, out):
    with ExitStack() as ctx:
        base = nc.sbuf_base + (-nc.sbuf_base) % 32

        def at(name, kib, shape, dt=F32):
            return nc.alloc_sbuf_tensor_at(name, [P] + shape, dt, offset=base + int(kib * 1024))

        def sem(name):
            return ctx.enter_context(nc.semaphore(name))

        raw = [at(f"raw{j}", 4 * j, [8, P]) for j in range(SLOTS)]
        w_hi = [at(f"w_hi{j}", 16 + 4 * j, [8, P], F32R) for j in range(SLOTS)]
        w_lo = [at(f"w_lo{j}", 32 + 4 * j, [8, P], F32R) for j in range(SLOTS)]
        modw = [at(f"modw{j}", 48 + 4 * j, [D]) for j in range(MOD_SLOTS)]
        c_row = at("c_row", 64, [3, D])
        x = at("x", 76, [KT, T])
        cols = at("cols", 84, [NCOLS])
        con = at("con", 86.5, [NCONS])
        mod = at("mod", 91, [MOD_TILES])
        mod_c = at("mod_c", 91.375, [2 * KT])
        mod0 = at("mod0", 91.5, [2 * KT, 2])
        small = at("small", 91.75, [448])
        W = 94

        ident = con[:, CON["ident"]:CON["ident"] + P]
        ones = con[:, CON["ones"]:CON["ones"] + P]

        def col(name, n=0, k=1):
            return cols[:, COL[name] + n:COL[name] + n + k]

        used = [0]

        def columns(n):
            used[0] += n
            assert used[0] <= 448
            return small[:, used[0] - n:used[0]]

        h_hi = at("h_hi", W, [KT, 2, T], F32R)
        h_lo = at("h_lo", W + 16, [KT, 2, T], F32R)
        u_hi = at("u_hi", W + 32, [KT, 2, T], F32R)
        u_lo = at("u_lo", W + 48, [KT, 2, T], F32R)
        XW = T + SCONV_TAPS
        xpad = at("xpad", W + 64, [KT, 2, XW])
        UW = T + CONV_TAPS - 1
        upad = at("upad", W + 80.25, [KT, UW])
        conv = at("conv", W + 89.25, [KT, T])
        ga = at("ga", W + 97.25, [KT, T])
        gb = at("gb", W + 105.25, [KT, T])
        ctxT = at("ctxT", W + 97.25, [KT, T])
        sq0 = at("sq0", W + 105.25, [KT, T])
        t0 = at("t0", W + 80.25, [8, T])
        stmp = at("stmp", W + 105.25, [4, 2, T])
        ya_hi = at("ya_hi", W + 80.25, [KT, T], F32R)
        ya_lo = at("ya_lo", W + 89.25, [KT, T], F32R)
        yb_hi = at("yb_hi", W + 97.25, [KT, T], F32R)
        yb_lo = at("yb_lo", W + 105.25, [KT, T], F32R)
        lnsq = at("lnsq", W, [KT, T])
        lnt = at("lnt", W + 8, [8, T])
        tt = at("tt", W, [2, 2, 2 * T])
        iu = at("iu", W + 8, [2, 2, 2 * T])
        rt = at("rt", W + 16, [2, 2, 2 * T])
        rec = at("rec", W + 24, [2, 2 * T])
        aa = at("aa", W + 28, [2, 2 * T])

        sq1 = at("sq1", W, [KT, T])
        h1_hi = at("h1_hi", W + 8, [KT, T], F32R)
        h1_lo = at("h1_lo", W + 16, [KT, T], F32R)
        t1 = at("t1", W + 24, [8, T])
        PW = GRID_W + 16
        ROWS = T // GRID_W
        opad = at("opad", W + 32, [16, ROWS, PW])
        og = at("og", W + 52, [16, T])
        d_hi = at("d_hi", W + 68, [16, T], F32R)
        d_lo = at("d_lo", W + 84, [16, T], F32R)
        win = [at("win0", W, [16, PW]), at("win1", W + 24, [16, PW])]
        pd = at("pd", W + 100, [4, T])
        vr1 = at("vr1", W + 100, [T])
        ytmp = at("ytmp", W + 104, [2, 2, T])
        y_hi = at("y_hi", W + 8, [16, T], F32R)
        y_lo = at("y_lo", W + 32, [16, T], F32R)

        ctx2T = at("ctx2T", W + 24, [KT, T])
        sqc = at("sqc", W, [KT, T])
        sq2 = at("sq2", W + 48, [KT, T])
        t2 = at("t2", W + 56, [8, T])
        vr = at("vr", W + 64, [4, T])
        h2_hi = at("h2_hi", W + 68, [2, KT, T], F32R)
        h2_lo = at("h2_lo", W + 84, [2, KT, T], F32R)
        Lg = at("Lg", W, [2, HEADS, 2, T])
        Kk = at("Kk", W + 16, [2, HEADS, 2, T])
        V = at("V", W + 32, [HEADS, 2, T])
        q = at("q", W + 40, [HEADS, T])
        og2 = at("og2", W + 44, [HEADS, T])
        u2 = at("u2", W + 48, [HEADS, T])
        v2 = at("v2", W + 52, [HEADS, T])
        tq = at("tq", W + 56, [HEADS, T])
        qi = at("qi", W + 60, [HEADS, T])
        ki = at("ki", W + 64, [HEADS, T])
        St = at("St", W + 76, [CHUNKS, HEADS, P])
        vtok = at("vtok", W + 92, [2, 2, HEADS, P])
        kdT = at("kdT", W + 100, [HEADS, 2, P])
        sc = at("sc", W + 104, [HEADS * 2, P])
        wsT = at("wsT", W + 108, [HEADS, P])
        bsr = at("bsr", W + 110, [HEADS * P])
        tri = at("tri", W + 112, [2, P], I32)
        ga2 = at("ga2", 48, [KT, T])
        gb2 = at("gb2", 56, [KT, T])
        osq = at("osq", W + 56, [HEADS, T])
        ors = at("ors", W + 60, [HEADS, T])
        o1 = at("o1", W + 64, [HEADS, T])
        vn = at("vn", W + 76, [HEADS, T])
        vsq = at("vsq", W + 80, [HEADS, T])
        lnv = at("lnv", W + 100, [4, T])
        vt = at("vt", W + 92, [2, HEADS, P])
        ob = at("ob", W + 96, [HEADS, T])
        oa_hi, oa_lo = at("oa_hi", W, [HEADS, T], F32R), at("oa_lo", W + 4, [HEADS, T], F32R)
        ob_hi, ob_lo = at("ob_hi", W + 8, [HEADS, T], F32R), at("ob_lo", W + 12, [HEADS, T], F32R)
        m_hi, m_lo = at("m_hi", W + 16, [KT, T], F32R), at("m_lo", W + 24, [KT, T], F32R)
        mt = at("mt", W + 32, [2, 2, 2, T])

        sq4 = at("sq4", W, [KT, T])
        t4 = at("t4", W + 8, [8, T])
        h3_hi, h3_lo = at("h3_hi", W + 32, [KT, T], F32R), at("h3_lo", W + 40, [KT, T], F32R)
        ff_hi, ff_lo = at("ff_hi", W + 48, [FT, T], F32R), at("ff_lo", W + 70, [FT, T], F32R)
        sa = at("sa", W + 92, [2, T])
        ff = at("ff", W + 94, [2, T])
        v4 = at("v4", W + 98, [2, T])
        sq5 = at("sq5", W, [KT, T])

        ps = [ctx.enter_context(nc.psum_tensor(f"ps{j}", [P, 2 * T], F32)) for j in range(SLOTS)]
        px = [ctx.enter_context(nc.psum_tensor(f"px{j}", [P, 2 * T], F32)) for j in range(4)]

        raw_in = [sem(f"raw_in{j}") for j in range(SLOTS)]
        mod0_used = [sem(f"mod0_used{j}") for j in range(SLOTS)]
        hi_ready = [sem(f"hi_ready{j}") for j in range(SLOTS)]
        lo_ready = [sem(f"lo_ready{j}") for j in range(SLOTS)]
        pe_done = [sem(f"pe_done{j}") for j in range(SLOTS)]
        ps_free = [sem(f"ps_free{j}") for j in range(SLOTS)]
        modw_in = [sem(f"modw_in{j}") for j in range(MOD_SLOTS)]
        modw_used = [sem(f"modw_used{j}") for j in range(MOD_SLOTS)]
        in_cc, in_con, in_x, in_crow = sem("in_cc"), sem("in_con"), sem("in_x"), sem("in_crow")
        cc_ready = sem("cc_ready")
        crow_ready = sem("crow_ready")
        sq_ready = sem("sq_ready")
        stat_done = sem("stat_done")
        var_ready = sem("var_ready")
        sd_ready = sem("sd_ready")
        opnd = sem("opnd")
        mod0_done = sem("mod0_done")
        softplus_in = sem("softplus_in")
        softplus_ex = sem("softplus_ex")
        lru_cols = sem("lru_cols")
        gates_pe = sem("gates_pe")
        gates_out = sem("gates_out")
        tanh_ready = sem("tanh_ready")
        root_ready = sem("root_ready")
        lru_free = sem("lru_free")
        pads_ready = sem("pads_ready")
        in_ctx2, in_sgu = sem("in_ctx2"), sem("in_sgu")
        lb_in, lb_ex = sem("lb_in"), sem("lb_ex")
        fk = sem("fk")
        logf = sem("logf")
        hx_dve, hx_act = sem("hx_dve"), sem("hx_act")
        hg_dve, hg_act, hg_pe = sem("hg_dve"), sem("hg_act"), sem("hg_pe")
        sg_dve, sg_act, sg_pe = sem("sg_dve"), sem("sg_act"), sem("sg_pe")
        silu_ready = sem("silu_ready")
        stored = sem("stored")
        x3_ready = sem("x3_ready")
        ln_sq, ln_norm, ln_silu = sem("ln_sq"), sem("ln_norm"), sem("ln_silu")
        dve_step = sem("dve_step")
        act_step = sem("act_step")
        out_done = sem("out_done")

        modA = [columns(KT), columns(KT)]
        modS = [columns(KT), columns(KT)]
        gate0 = columns(KT)
        sc2 = [columns(KT), columns(KT)]
        sh2 = [columns(KT), columns(KT)]
        gate2, sc3, sh3, gate3 = columns(KT), columns(KT), columns(KT), columns(KT)
        tots, bls, mids, dec = columns(8), columns(16), columns(16), columns(16)
        lru_c = columns(2 * KT)
        lam_t = [columns(2 * KT) for _ in range(4)]
        ccs = columns(2 * KT)
        warm = columns(1)
        sc1, gate1 = columns(KT), columns(KT)
        shift1 = columns(KT)
        lb_t = [columns(2 * HEADS) for _ in range(3)]
        lb, oml, noml = (columns(2 * HEADS) for _ in range(3))

        block = ctx.enter_context(nc.Block())

        OPND, n = {}, 0
        for name, tiles in (("h0", 16), ("u", 8), ("ya", 8), ("yb", 8), ("h1", 8), ("d", 4), ("y", 8),
                            ("hc2", 8), ("h2", 8), ("oa", 1), ("ob", 1), ("m", 4), ("h3", 8), ("ff", FT)):
            OPND[name] = n
            n += tiles

        @block.sync
        def _(sp):
            sp.dma_start(ccs, ins["c_cols"]).then_inc(in_cc, 16)
            for j in range(SLOTS):
                sp.dma_start(raw[j][:], ins["mod0_w"][j]).then_inc(raw_in[j], 16)
            sp.dma_start(ctxT[:], ins["ctxT"]).then_inc(in_x, 16)
            sp.dma_start(x[:], ins["xT"]).then_inc(in_x, 16)
            sp.dma_start(cols[:], ins["cols"]).then_inc(in_con, 16)
            sp.dma_start(con[:], ins["con"]).then_inc(in_con, 16)
            with sp.Fori(1, MOD0_ROUNDS) as r:
                for j in range(SLOTS):
                    sp.wait_ge(mod0_used[j], r)
                    sp.dma_start(raw[j][:], ins["mod0_w"][r * SLOTS + j]).then_inc(raw_in[j], 16)
            for n in range(3):
                sp.dma_start(c_row[:, n, :], ins["c_rows"][n:n + 1, :].partition_broadcast(P)).then_inc(in_crow, 16)
            for j in range(SLOTS):
                sp.wait_ge(mod0_used[j], MOD0_ROUNDS)
                sp.dma_start(raw[j][:], ins["stream"][j]).then_inc(raw_in[j], 16)

            def mod_group(g):
                for s in range(MOD_SLOTS):
                    if g:
                        sp.wait_ge(modw_used[s], g)
                    sp.dma_start(modw[s][:], ins["mod_w"][g * MOD_SLOTS + s]).then_inc(modw_in[s], 16)

            def rounds(first, end):
                with sp.Fori(first, end) as r:
                    for j in range(SLOTS):
                        sp.wait_ge(lo_ready[j], r)
                        sp.dma_start(raw[j][:], ins["stream"][r * SLOTS + j]).then_inc(raw_in[j], 16)

            mod_group(0)
            rounds(1, 4)
            mod_group(1)
            rounds(4, BASE["ya"])
            mod_group(2)
            rounds(BASE["ya"], BASE["od_u"])
            mod_group(3)
            rounds(BASE["od_u"], BASE["od_u"] + 2)
            for g in range(4, 9):
                mod_group(g)
            for n in range(4):
                if n < 3:
                    rounds(BASE["od_u"] + 2 + 2 * n, BASE["od_u"] + 4 + 2 * n)
                mod_group(9 + n)
            sp.wait_ge(opnd, OPND["d"] + 4)
            sp.dma_start(ctx2T[:], ins["ctx2T"]).then_inc(in_ctx2, 16)
            rounds(BASE["grp"], BASE["oda"])
            mod_group(13)
            rounds(BASE["oda"], BASE["f"])
            mod_group(14)
            rounds(BASE["f"], BASE["i"])
            for g in range(15, MOD_TILES // MOD_SLOTS):
                mod_group(g)
            sp.wait_ge(ps_free[3], BASE["f"])
            sp.dma_start(wsT[:], ins["wsT"]).then_inc(in_sgu, 16)
            sp.dma_start(bsr[0:1, :], ins["b_s"]).then_inc(in_sgu, 16)
            sp.dma_start(tri[:], ins["tri"]).then_inc(in_sgu, 16)
            rounds(BASE["i"], ROUNDS)
            for k in range(KT):
                sp.wait_ge(stored, k + 1)
                sp.dma_start(out[:, k, :], x[:, k, :]).then_inc(out_done, 16)
            sp.wait_ge(out_done, 16 * KT)

        @block.gpsimd
        def _(pool):
            with pool.Fori(0, ROUNDS) as r:
                for j in range(SLOTS):
                    pool.wait_ge(hi_ready[j], r + 1)
                    pool.tensor_tensor(w_lo[j][:], raw[j][:], w_hi[j][:].bitcast(F32),
                                       ALU.subtract).then_inc(lo_ready[j], 1)

        @block.tensor
        def _(pe):
            pe.wait_ge(cc_ready, 1)
            with pe.Fori(0, MOD0_ROUNDS) as r:
                for j in range(SLOTS):
                    pe.wait_ge(raw_in[j], r * 16 + 16)
                    for k in range(KT):
                        last = pe.matmul(px[3][:, bass.ds(r * 2 * SLOTS + 2 * j, 2)], raw[j][:, k, :],
                                         ccs[:, 2 * k:2 * k + 2], start=(k == 0), stop=(k == KT - 1))
                    last.then_inc(mod0_used[j], 1)

            def stats(bank, squares, ready, signal=sq_ready, width=T, tiles=KT):
                for k in range(tiles):
                    pe.wait_ge(signal, ready + k + 1)
                    last = pe.matmul(bank[:, 0:width], ones, squares(k), start=(k == 0),
                                     stop=(k == tiles - 1))
                last.then_inc(stat_done, 1)

            def stream(name, hi, lo, width, opnds, tiles=KT):
                def one_round(i, first):
                    for j in range(SLOTS):
                        pe.wait_ge(lo_ready[j], i + (BASE[name] + 1))
                        if not first:
                            pe.wait_ge(ps_free[j], i + BASE[name])
                        for k in range(tiles):
                            if j == 0 and opnds is not None:
                                pe.wait_ge(opnd, opnds + k + 1)
                            pe.matmul(ps[j][:, 0:width], w_hi[j][:, k, :], hi(k), start=(k == 0), stop=False)
                            pe.matmul(ps[j][:, 0:width], w_hi[j][:, k, :], lo(k), start=False, stop=False)
                            last = pe.matmul(ps[j][:, 0:width], w_lo[j][:, k, :], hi(k), start=False,
                                             stop=(k == tiles - 1))
                        last.then_inc(pe_done[j], 1)

                peeled = 1 if BASE[name] == 0 else 0
                if peeled:
                    one_round(0, True)
                with pe.Fori(peeled, ROUNDS_OF[name]) as i:
                    one_round(i, False)

            pe.wait_ge(in_con, 32)
            stats(px[0], lambda k: sq0[:, k, :], 0)
            stats(px[1], lambda k: sq0[:, k, :], KT)
            both = (lambda k: h_hi[:, k, :, :], lambda k: h_lo[:, k, :, :])
            own = (lambda k: h_hi[:, k, 1, :], lambda k: h_lo[:, k, 1, :])
            stream("xb", *both, 2 * T, OPND["h0"] + KT)
            stream("vavg", *own, T, None)
            stream("ga", *own, T, None)
            stream("gb", *own, T, None)

            stats(px[0], lambda k: conv[:, k, :], 2 * KT)
            stats(px[1], lambda k: lnsq[:, k, :], 0, ln_sq)

            pe.wait_ge(opnd, OPND["u"] + KT)
            pe.wait_ge(var_ready, 3)
            for j in range(SLOTS):
                pe.wait_ge(lo_ready[j], BASE["gates"] + 1)
                for e in range(2):
                    head = 2 * j + e
                    banks = px if e else ps
                    if head >= 2:
                        pe.wait_ge(gates_out, 4 * (head - 1))
                    else:
                        for b in range(SLOTS):
                            pe.wait_ge(ps_free[b], BASE["gates"])
                    for b in range(4):
                        k = 4 * e + b
                        o = banks[b][:, :]
                        pe.matmul(o, w_hi[j][:, k, :], u_hi[:, head, :, :], start=True, stop=False)
                        pe.matmul(o, w_hi[j][:, k, :], u_lo[:, head, :, :], start=False, stop=False)
                        last = pe.matmul(o, w_lo[j][:, k, :], u_hi[:, head, :, :], start=False, stop=True)
                        if e == 0 or b < 3:
                            last.then_inc(gates_pe, 1)
                    if e == 1:
                        last.then_inc(pe_done[j], 1)
            stream("ya", lambda k: ya_hi[:, k, :], lambda k: ya_lo[:, k, :], T, OPND["ya"])
            stream("yb", lambda k: yb_hi[:, k, :], lambda k: yb_lo[:, k, :], T, OPND["yb"])

            stats(px[0], lambda k: sq1[:, k, :], 3 * KT)
            h1 = (lambda k: h1_hi[:, k, :], lambda k: h1_lo[:, k, :])
            stream("od_u", *h1, T, OPND["h1"])
            stream("od_g", *h1, T, None)

            def pair_stream(name, hi, lo, ready):
                with pe.Fori(0, ROUNDS_OF[name]) as i:
                    for j in range(SLOTS):
                        pe.wait_ge(lo_ready[j], i + (BASE[name] + 1))
                        pe.wait_ge(ps_free[j], i + BASE[name])
                        ready(i, j)
                        for e in range(2):
                            o = ps[j][:, e * T:(e + 1) * T]
                            for k in range(4):
                                pe.matmul(o, w_hi[j][:, 4 * e + k, :], hi(i, j, k), start=(k == 0), stop=False)
                                pe.matmul(o, w_hi[j][:, 4 * e + k, :], lo(i, j, k), start=False, stop=False)
                                last = pe.matmul(o, w_lo[j][:, 4 * e + k, :], hi(i, j, k), start=False, stop=(k == 3))
                        last.then_inc(pe_done[j], 1)

            pair_stream("grp", lambda i, j, k: d_hi[:, i * 8 + (4 * (j // 2) + k), :],
                        lambda i, j, k: d_lo[:, i * 8 + (4 * (j // 2) + k), :],
                        lambda i, j: pe.wait_ge(opnd, i * 2 + (OPND["d"] + 1 + j // 2)))
            stats(px[1], lambda k: sqc[:, k, :], 4 * KT)
            for name, k0 in (("oda", 0), ("odb", 8)):
                pe.wait_ge(opnd, OPND["y"] + (4 if k0 == 0 else 8))
                stream(name, lambda k: y_hi[:, k0 + k, :], lambda k: y_lo[:, k0 + k, :], T, None)

            stats(px[0], lambda k: sq2[:, k, :], 5 * KT)
            stats(px[2], lambda k: sqc[:, k, :], 6 * KT)
            both2 = (lambda k: h2_hi[:, :, k, :], lambda k: h2_lo[:, :, k, :])
            own2 = (lambda k: h2_hi[:, 0, k, :], lambda k: h2_lo[:, 0, k, :])
            stream("f", *both2, 2 * T, OPND["h2"])
            stream("i", *both2, 2 * T, None)
            for s in range(2):
                for n in range(2):
                    for h in range(HEADS):
                        if s == 0 and n == 0:
                            pe.wait_ge(ps_free[h], BASE["i"] + 1)
                        last = pe.transpose(px[2 * s + n][:, h * P:(h + 1) * P], V[:, h, s, n * P:(n + 1) * P], ident)
                    last.then_inc(hg_pe, 1)
            stream("q", *own2, T, None)
            stream("uvo", *own2, T, None)

            def direction(d):
                A, B, C = 4 + 4 * d, 9 * d, 0

                def keys(s):
                    for n in range(2):
                        pe.wait_ge(hg_act, 4 + 4 * d)
                        for h in range(2):
                            for tile in range(2):
                                last = pe.transpose(px[n][:, (2 * h + tile) * P:(2 * h + tile + 1) * P],
                                                    Kk[:, d, 2 * n + h, s, tile * P:(tile + 1) * P], ident)
                        last.then_inc(hg_pe, 1)

                pe.wait_ge(hg_dve, B + 1)
                keys(1)
                pe.wait_ge(hg_act, A + 2)
                for h in range(HEADS):
                    for tile in range(2):
                        last = pe.matmul(px[0][:, h * P:(h + 1) * P], kdT[:, h, tile, :], vtok[:, 1, tile, h, :],
                                         start=(tile == 0), stop=(tile == 1))
                last.then_inc(hg_pe, 1)
                pe.wait_ge(hg_dve, B + 5)
                keys(0)
                pe.wait_ge(hg_act, A + 4)
                order = (0, 1, 2) if d == 0 else (3, 2, 1)
                for n, c in enumerate(order):
                    if n == 2:
                        pe.wait_ge(hg_dve, B + 6)
                    rows = slice((c % 2) * CHUNK, (c % 2 + 1) * CHUNK)
                    for h in range(HEADS):
                        last = pe.matmul(px[n % 2][:, h * P:(h + 1) * P], kdT[rows, h, c // 2, :],
                                         vtok[rows, 0, c // 2, h, :], start=True, stop=True)
                    last.then_inc(hg_pe, 1)
                pe.wait_ge(hg_dve, B + 8)
                for h in range(HEADS):
                    for tile in range(2):
                        t = slice(tile * P, (tile + 1) * P)
                        r = 2 * (h % 2) + tile
                        last = pe.matmul(px[h // 2][:, r * P:(r + 1) * P], ki[:, h, t], qi[:, h, t], start=True,
                                         stop=True)
                last.then_inc(hg_pe, 1)
                pe.wait_ge(hg_dve, B + 9)
                for h in range(HEADS):
                    for tile in range(2):
                        o = px[2 + h // 2][:, (h % 2) * T + tile * P:(h % 2) * T + (tile + 1) * P]
                        pe.matmul(o, vtok[:, 0, tile, h, :], sc[:, 2 * h + tile, :],
                                  start=(d == 0 and h % 2 == 0 and tile == 0), stop=False, skip_group_check=True)
                    for c in range(CHUNKS):
                        t = slice(c * CHUNK, (c + 1) * CHUNK)
                        o = px[2 + h // 2][:, (h % 2) * T + c * CHUNK:(h % 2) * T + (c + 1) * CHUNK]
                        last = pe.matmul(o, St[:, c, h, :], tq[:, h, t], start=False, stop=True,
                                         skip_group_check=True)
                last.then_inc(hg_pe, 1)

            direction(0)
            stream("ga2", *own2, T, None)
            direction(1)
            stream("gb2", *own2, T, None)

            for n in range(2):
                pe.wait_ge(sg_act, 1)
                pe.matmul(px[n][:, :], ones, osq[:, 2 * n:2 * n + 2, :], start=True, stop=True).then_inc(sg_pe, 1)
            pe.wait_ge(var_ready, 8)
            pe.wait_ge(sg_act, 2)
            for n, src in ((0, v2), (1, vsq)):
                for g in range(HEADS):
                    last = pe.matmul(px[n][:, 0:T], ones, src[:, g, :], start=(g == 0), stop=(g == HEADS - 1))
                last.then_inc(sg_pe, 1)
            pe.wait_ge(sg_dve, 1)
            for c in range(2):
                for g in range(HEADS):
                    last = pe.transpose(px[c][:, g * P:(g + 1) * P], vn[:, g, c * P:(c + 1) * P], ident)
                last.then_inc(sg_pe, 1)
            pe.wait_ge(sg_act, 4)
            pe.wait_ge(in_sgu, 48)
            for g in range(HEADS):
                for c in range(2):
                    o = px[g // 2][:, (g % 2) * T + c * P:(g % 2) * T + (c + 1) * P]
                    pe.matmul(o, vt[:, c, g, :], wsT[:, g, :], start=True, stop=False)
                    last = pe.matmul(o, ones[0:1, :], bsr[0:1, g * P:(g + 1) * P], start=False, stop=True)
            last.then_inc(sg_pe, 1)

            def ab(part):
                return lambda i, j, k: ((oa_hi, oa_lo), (ob_hi, ob_lo))[j % 2][part][:, k, :]

            pair_stream("pab", ab(0), ab(1), lambda i, j: pe.wait_ge(opnd, OPND["oa"] + 1 + j % 2))
            pe.wait_ge(opnd, OPND["m"] + 4)
            stream("wo", lambda k: m_hi[:, k, :], lambda k: m_lo[:, k, :], T, None)
            stats(px[0], lambda k: sq4[:, k, :], 7 * KT)
            stream("up", lambda k: h3_hi[:, k, :], lambda k: h3_lo[:, k, :], T, OPND["h3"])
            for name, k0, n in (("dna", 0, 8), ("dnb", 8, 8), ("dnc", 16, 6)):
                pe.wait_ge(opnd, OPND["ff"] + k0 + n)
                stream(name, lambda k: ff_hi[:, k0 + k, :], lambda k: ff_lo[:, k0 + k, :], T, None, n)
            stats(px[0], lambda k: sq5[:, k, :], 8 * KT)

        @block.scalar
        def _(act):
            S = Steps(act, act_step)

            def hi(r, j):
                act.wait_ge(raw_in[j], (r + (MOD0_ROUNDS + 1)) * 16)
                act.activation(w_hi[j][:], raw[j][:], ACT.Copy).then_inc(hi_ready[j], 1)

            def phase(name, evac=None, last_round=False):
                n = ROUNDS_OF[name] - (1 if last_round else 0)
                if n:
                    with act.Fori(0, n) as i:
                        for j in range(SLOTS):
                            act.wait_ge(pe_done[j], i + (BASE[name] + 1))
                            if evac:
                                evac(i, j)
                            hi(i + (BASE[name] + 1), j)
                if last_round:
                    for j in range(SLOTS):
                        act.wait_ge(pe_done[j], BASE[name] + n + 1)
                        if evac:
                            evac(n, j)

            act.wait_ge(in_cc, 16)
            act.activation(ccs, ccs, ACT.Silu).then_inc(cc_ready, 1)
            act.wait_ge(in_x, 32)
            for k in range(KT):
                act.activation(sq0[:, k, :], ctxT[:, k, :], ACT.Square).then_inc(sq_ready, 1)
            act.wait_ge(stat_done, 1)
            for k in range(KT):
                act.activation(sq0[:, k, :], x[:, k, :], ACT.Square).then_inc(sq_ready, 1)
            act.wait_ge(softplus_in, 1)
            act.activation(lam_t[0], lam_t[0], ACT.Exp).then_inc(softplus_ex, 1)
            for n in range(2):
                act.wait_ge(var_ready, n + 1)
                act.activation(t0[:, n, :], t0[:, n, :], ACT.Sqrt).then_inc(sd_ready, 1)
            act.wait_ge(in_crow, 48)
            act.activation(c_row[:], c_row[:], ACT.Silu).then_inc(crow_ready, 1)
            for j in range(SLOTS):
                hi(0, j)

            def xb(i, j):
                act.activation(xpad[:, i * SLOTS + j, :, SCONV_LEFT:SCONV_LEFT + T],
                               ps[j][:].rearrange("p (s t) -> p s t", s=2), ACT.Copy).then_inc(ps_free[j], 1)

            def vavg(i, j):
                tile = i * 2 + j // 2
                if j % 2 == 0:
                    act.activation(upad[:, tile, CONV_LEFT:CONV_LEFT + T], ps[j][:, 0:T], ACT.Copy) \
                       .then_inc(ps_free[j], 1)
                else:
                    act.activation(conv[:, tile, :], ps[j][:, 0:T], ACT.Sigmoid).then_inc(ps_free[j], 1)

            def silu_to(dst):
                def evac(i, j):
                    act.activation(dst[:, i * SLOTS + j, :], ps[j][:, 0:T], ACT.Silu).then_inc(ps_free[j], 1)
                return evac

            phase("xb", xb)
            phase("vavg", vavg)
            phase("ga", silu_to(ga))
            phase("gb", silu_to(gb))

            for k in range(KT):
                act.wait_ge(sq_ready, 2 * KT + k + 1)
                act.activation(lnsq[:, k, :], conv[:, k, :], ACT.Square).then_inc(ln_sq, 1)
            act.wait_ge(var_ready, 3)
            act.activation(lnt[:, 3, :], lnt[:, 3, :], ACT.Sqrt).then_inc(sd_ready, 1)
            for k in range(KT):
                act.wait_ge(ln_norm, k + 1)
                act.activation(conv[:, k, :], conv[:, k, :], ACT.Silu, scale=col("ev_ln_g", k),
                               bias=col("ev_ln_b", k)).then_inc(ln_silu, 1)

            for head in range(KT):
                b = head % 2
                banks = px if head % 2 else ps
                if head >= 2:
                    act.wait_ge(lru_free, head - 1)
                for g in range(4):
                    d, is_i = g // 2, g % 2
                    if head % 2 and g == 3:
                        act.wait_ge(pe_done[head // 2], BASE["gates"] + 1)
                    else:
                        act.wait_ge(gates_pe, 7 * (head // 2) + 4 * (head % 2) + g + 1)
                    dst = iu if is_i else tt
                    bias = col("ev_b_i" if is_i else "ev_b_r", KT * d + head)
                    a = act.activation(dst[:, b, d, :], banks[g][:, :], ACT.Sigmoid, bias=bias)
                    a.then_inc(gates_out, 1)
                act.wait_ge(gates_out, 4 * head + 4)
                act.wait_ge(lru_cols, 1)
                for d in range(2):
                    act.activation(tt[:, b, d, :], tt[:, b, d, :], ACT.Tanh,
                                   scale=lru_c[:, KT * d + head:KT * d + head + 1]).then_inc(tanh_ready, 1)
                act.wait_ge(tanh_ready, 2 * head + 2)
                act.activation(rt[:, b], tt[:, b], ACT.Sqrt).then_inc(root_ready, 1)
                if head % 2:
                    hi(BASE["gates"] + 1, head // 2)
            for j in range(SLOTS):
                act.sem_inc(ps_free[j], 1)
            def squares(name, dst):
                def evac(i, j):
                    act.wait_ge(ps_free[j], i + (BASE[name] + 1))
                    act.activation(dst[:, i * SLOTS + j, :], x[:, i * SLOTS + j, :], ACT.Square).then_inc(sq_ready, 1)
                return evac

            def phase_sq(name, dst, last_round=False):
                n = ROUNDS_OF[name] - (1 if last_round else 0)
                with act.Fori(0, n) as i:
                    for j in range(SLOTS):
                        act.wait_ge(pe_done[j], i + (BASE[name] + 1))
                        hi(i + (BASE[name] + 1), j)
                    for j in range(SLOTS):
                        squares(name, dst)(i, j)
                if last_round:
                    for j in range(SLOTS):
                        squares(name, dst)(n, j)

            phase("ya")
            phase_sq("yb", sq1)

            def sqrt_of(n, t):
                act.activation(warm, warm, ACT.Sqrt).then_inc(act_step, 1)
                S.n += 1
                act.wait_ge(var_ready, n)
                S.sync()
                act.activation(t, t, ACT.Sqrt).then_inc(sd_ready, 1)

            sqrt_of(4, t1[:, 0, :])

            def od_u(i, j):
                act.activation(opad[:, i * SLOTS + j, :, 8:8 + GRID_W],
                               ps[j][:, 0:T].rearrange("p (r c) -> p r c", c=GRID_W), ACT.Copy) \
                   .then_inc(ps_free[j], 1)

            act.wait_ge(pads_ready, 1)
            phase("od_u", od_u)
            phase("od_g", silu_to(og))
            phase("grp")
            act.wait_ge(in_ctx2, 16)
            for k in range(KT):
                act.activation(sqc[:, k, :], ctx2T[:, k, :], ACT.Square).then_inc(sq_ready, 1)
            sqrt_of(5, vr[:, 0, :])
            phase("oda")
            phase_sq("odb", sq2)
            sqrt_of(6, vr[:, 1, :])
            for k in range(KT):
                act.wait_ge(x3_ready, k + 1)
                act.activation(sqc[:, k, :], x[:, k, :], ACT.Square).then_inc(sq_ready, 1)
            sqrt_of(7, vr[:, 2, :])
            act.wait_ge(lb_in, 1)
            act.activation(lb_t[0], lb_t[0], ACT.Exp).then_inc(lb_ex, 1)
            act.activation(lb_t[1], lb_t[1], ACT.Exp).then_inc(lb_ex, 1)

            def f_evac(i, j):
                act.activation(Lg[:, i, j, :, :], ps[j][:].rearrange("p (s t) -> p s t", s=2), ACT.Sigmoid) \
                   .then_inc(ps_free[j], 1)

            def i_evac(i, j):
                act.activation(V[:, j, :, :], ps[j][:].rearrange("p (s t) -> p s t", s=2), ACT.Copy) \
                   .then_inc(ps_free[j], 1)

            phase("f", f_evac)
            phase("i", i_evac)
            for n in range(4):
                act.wait_ge(hg_pe, n + 1)
                act.activation(vtok[:, n // 2, n % 2, :, :], px[n][:].rearrange("p (h e) -> p h e", h=HEADS),
                               ACT.Copy).then_inc(hg_act, 1)
            for d in range(2):
                act.wait_ge(fk, d + 1)
                act.activation(Lg[:, d], Lg[:, d], ACT.Ln).then_inc(logf, 1)

            def exps(d):
                act.wait_ge(hx_dve, 2 * d + 1)
                for h in range(HEADS):
                    act.activation(Lg[:, d, h, 1, :], Lg[:, d, h, 1, :], ACT.Exp, scale=-1.0,
                                   bias=tots[:, HEADS * d + h:HEADS * d + h + 1]).then_inc(hx_act, 1)
                act.activation(ki[:], tq[:], ACT.Exp, scale=-1.0).then_inc(hx_act, 1)
                act.activation(qi[:], tq[:], ACT.Exp).then_inc(hx_act, 1)
                act.activation(dec, bls, ACT.Exp).then_inc(hx_act, 1)
                act.wait_ge(hx_act, 9 * d + 6)
                act.activation(tq[:], Lg[:, d, :, 0, :], ACT.Exp).then_inc(hx_act, 1)
                act.wait_ge(hx_dve, 2 * d + 2)
                act.activation(Lg[:, d, :, 0, :], Lg[:, d, :, 0, :], ACT.Exp).then_inc(hx_act, 1)

            def keys_out(d):
                for s in range(2):
                    if s:
                        act.wait_ge(hg_pe, 4 + 10 * d + 3)
                    for n in range(2):
                        act.wait_ge(hg_pe, 4 + 10 * d + 3 * s + n + 1)
                        act.activation(kdT[:, 2 * n:2 * n + 2, :, :],
                                       px[n][:].rearrange("p (h t d) -> p h t d", h=2, t=2), ACT.Copy) \
                           .then_inc(hg_act, 1)

            def q_evac(i, j):
                act.activation(q[:, j, :], ps[j][:, 0:T], ACT.Copy).then_inc(ps_free[j], 1)

            phase("q", q_evac)
            exps(0)
            for n, (dst, func) in enumerate(((u2, ACT.Gelu_apprx_tanh), (v2, ACT.Gelu_apprx_tanh), (og2, ACT.Silu))):
                for j in range(SLOTS):
                    act.wait_ge(pe_done[j], BASE["uvo"] + n + 1)
                    act.activation(dst[:, j, :], ps[j][:, 0:T], func).then_inc(ps_free[j], 1)
                    hi(BASE["uvo"] + n + 1, j)

            def sigmoid_to(dst):
                def evac(i, j):
                    act.activation(dst[:, i * SLOTS + j, :], ps[j][:, 0:T], ACT.Sigmoid).then_inc(ps_free[j], 1)
                return evac

            keys_out(0)
            phase("ga2", sigmoid_to(ga2))
            act.wait_ge(hg_pe, 14)
            exps(1)
            keys_out(1)
            phase("gb2", sigmoid_to(gb2))
            act.wait_ge(hg_pe, 24)
            for n in range(2):
                a = act.activation(osq[:, 2 * n:2 * n + 2, :], px[2 + n][:].rearrange("p (h t) -> p h t", h=2),
                                   ACT.Square)
                if n:
                    a.then_inc(sg_act, 1)
                else:
                    S.do(a)
            S.sync()
            act.activation(vsq[:], v2[:], ACT.Square).then_inc(sg_act, 1)
            sqrt_of(8, ors[:])
            sqrt_of(9, lnv[:, 3, :])
            for c in range(2):
                act.wait_ge(sg_pe, 5 + c)
                act.activation(vt[:, c, :, :], px[c][:].rearrange("p (g e) -> p g e", g=HEADS), ACT.Copy) \
                   .then_inc(sg_act, 1)
            phase("pab")
            phase_sq("wo", sq4)
            sqrt_of(10, v4[:, 0, :])

            def up(i, j):
                if j % 2 == 0:
                    act.wait_ge(ps_free[j + 1], i + BASE["up"])
                    act.activation(sa[:, j // 2, :], ps[j][:, 0:T], ACT.Silu).then_inc(ps_free[j], 1)

            phase("up", up)
            phase("dna")
            phase("dnb")
            phase_sq("dnc", sq5, last_round=True)
            sqrt_of(11, v4[:, 0, :])

        @block.vector
        def _(v):
            S = Steps(v, dve_step)

            def tt_(o, a, b, op):
                return v.tensor_tensor(o, a, b, op)

            def modulate(tiles, src, rstd, scale, shift, tmp, hi, lo):
                for s in range(tiles + 3):
                    if s < tiles:
                        if s >= 1:
                            S.sync()
                        S.do(tt_(tmp[:, s % 4, :], src(s), rstd, ALU.mult))
                    k = s - 1
                    if 0 <= k < tiles:
                        S.sync(S.n - (1 if s < tiles else 0))
                        S.do(v.tensor_scalar(tmp[:, 4 + k % 4, :], tmp[:, k % 4, :], scale(k), shift(k), ALU.mult,
                                             ALU.add))
                    k = s - 2
                    if 0 <= k < tiles:
                        S.do(v.tensor_copy(hi(k), tmp[:, 4 + k % 4, :]))
                    k = s - 3
                    if 0 <= k < tiles:
                        S.sync(S.n - (1 if s - 2 < tiles else 0))
                        v.tensor_tensor(lo(k), tmp[:, 4 + k % 4, :], hi(k).bitcast(F32), ALU.subtract) \
                         .then_inc(opnd, 1)

            def mod_tiles(g, row):
                for s in range(MOD_SLOTS):
                    q = g * MOD_SLOTS + s
                    v.wait_ge(modw_in[s], 16 * (g + 1))
                    v.scalar_tensor_tensor(out=modw[s][:], in0=modw[s][:], scalar=1.0, in1=c_row[:, row, :],
                                           op0=ALU.mult, op1=ALU.mult,
                                           accum_out=mod[:, q:q + 1]).then_inc(modw_used[s], 1)

            v.wait_ge(in_con, 32)
            S.do(v.memset(xpad[:, :, :, 0:SCONV_LEFT], 0.0))
            S.do(v.memset(xpad[:, :, :, SCONV_LEFT + T:XW], 0.0))
            S.do(v.memset(warm, 1.0))

            lam = col("ev_lam", 0, 2 * KT)
            S.do(v.tensor_scalar(lam_t[1], lam, -1.0, None, ALU.mult))
            S.sync()
            v.tensor_tensor(lam_t[0], lam, lam_t[1], ALU.min).then_inc(softplus_in, 1)
            v.wait_ge(softplus_ex, 1)
            S.do(v.tensor_scalar(lam_t[2], lam_t[0], 2.0, None, ALU.add))
            S.sync()
            S.do(v.reciprocal(lam_t[2], lam_t[2]))
            S.sync()
            S.do(tt_(lam_t[0], lam_t[0], lam_t[2], ALU.mult))
            S.sync()
            S.do(tt_(lam_t[2], lam_t[0], lam_t[0], ALU.mult))
            S.sync()
            S.do(v.tensor_scalar(lam_t[3], lam_t[2], 1 / 17, 1 / 15, ALU.mult, ALU.add))
            for m in (13, 11, 9, 7, 5, 3, 1):
                S.sync()
                S.do(tt_(lam_t[3], lam_t[3], lam_t[2], ALU.mult))
                S.sync()
                S.do(v.tensor_scalar(lam_t[3], lam_t[3], 1 / m, None, ALU.add))
            S.sync()
            S.do(tt_(lam_t[3], lam_t[3], lam_t[0], ALU.mult))
            S.do(v.tensor_scalar(lam_t[1], lam_t[1], 0.0, 4.0, ALU.max, ALU.mult))
            S.sync()
            v.scalar_tensor_tensor(out=lru_c, in0=lam_t[3], scalar=8.0, in1=lam_t[1], op0=ALU.mult,
                                   op1=ALU.add).then_inc(lru_cols, 1)

            for j in range(SLOTS):
                v.wait_ge(mod0_used[j], MOD0_ROUNDS)
            for w in range(2):
                S.do(tt_(mod0[:, :, w], px[3][:, w:4 * KT:2], col("mod_b", 0, 2 * KT), ALU.add))
            S.sync()
            for w in range(2):
                S.do(v.tensor_scalar(modS[w], mod0[:, 0:KT, w], 1.0, None, ALU.mult))
                S.do(v.scalar_tensor_tensor(out=modA[w], in0=mod0[:, KT:2 * KT, w], scalar=1.0,
                                            in1=col("norm_g", 0, KT), op0=ALU.add, op1=ALU.mult))

            v.wait_ge(stat_done, 1)
            v.tensor_scalar(t0[:, 0, :], px[0][:, 0:T], 1.0 / D, EPS6, ALU.mult, ALU.add).then_inc(var_ready, 1)
            v.wait_ge(stat_done, 2)
            v.tensor_scalar(t0[:, 1, :], px[1][:, 0:T], 1.0 / D, EPS6, ALU.mult, ALU.add).then_inc(var_ready, 1)
            rs = [conv[:, n, :] for n in range(2)]
            for n in range(2):
                v.wait_ge(sd_ready, n + 1)
                S.do(v.reciprocal(rs[n], t0[:, n, :]))
            S.sync()
            v.wait_ge(sq_ready, 2 * KT)
            for n, (src, w) in enumerate(((ctxT, 1), (x, 0))):
                modulate(KT, lambda k: src[:, k, :], rs[n], lambda k: modA[w][:, k:k + 1],
                         lambda k: modS[w][:, k:k + 1], t0, lambda k: h_hi[:, k, n, :], lambda k: h_lo[:, k, n, :])
            v.wait_ge(opnd, OPND["h0"] + 2 * KT)
            S.do(v.memset(upad[:, :, 0:CONV_LEFT], 0.0))
            S.do(v.memset(upad[:, :, CONV_LEFT + T:UW], 0.0))

            for i in S.loop(ROUNDS_OF["xb"], 5 * SLOTS):
                for j in range(SLOTS):
                    tile = i * SLOTS + j
                    v.wait_ge(ps_free[j], i + 1)
                    tmp = stmp[:, j]

                    def tap(n):
                        c0 = COL["ev_sconv_w"] + KT * n
                        return xpad[:, tile, :, n:n + T], cols[:, bass.ds(tile + c0, 1)]

                    src, w = tap(0)
                    S.do(v.tensor_scalar(tmp, src, w, cols[:, bass.ds(tile + COL["ev_sconv_b"], 1)], ALU.mult,
                                         ALU.add))
                    for n in (1, 3):
                        src, w = tap(n)
                        S.sync()
                        S.do(v.scalar_tensor_tensor(out=tmp, in0=src, scalar=w, in1=tmp, op0=ALU.mult, op1=ALU.add))
                    src, w = tap(SCONV_LEFT)
                    S.sync()
                    S.do(v.scalar_tensor_tensor(out=src, in0=src, scalar=w, in1=tmp, op0=ALU.mult, op1=ALU.add))
                    S.sync()
                    S.do(v.tensor_copy(u_hi[:, tile], src))
                    S.sync()
                    v.tensor_tensor(u_lo[:, tile], src, u_hi[:, tile].bitcast(F32), ALU.subtract).then_inc(opnd, 1)

            v.wait_ge(crow_ready, 1)
            mod_tiles(0, 0)
            mod_tiles(1, 0)

            for i in S.loop(ROUNDS_OF["vavg"], 2 * (1 + CONV_TAPS) - 2):
                for e in range(2):
                    tile = i * 2 + e
                    v.wait_ge(ps_free[2 * e], i + (BASE["vavg"] + 1))
                    v.wait_ge(ps_free[2 * e + 1], i + (BASE["vavg"] + 1))
                    mid = upad[:, tile, CONV_LEFT:CONV_LEFT + T]
                    S.do(tt_(mid, mid, conv[:, tile, :], ALU.mult))
                for n in range(CONV_TAPS):
                    for e in range(2):
                        tile = i * 2 + e
                        src = upad[:, tile, n:n + T]
                        w = cols[:, bass.ds(tile + (COL["ev_conv_w"] + KT * n), 1)]
                        S.sync(S.n if n == CONV_TAPS - 1 and e else S.n - 1)
                        if n == 0:
                            S.do(v.tensor_scalar(conv[:, tile, :], src, w,
                                                 cols[:, bass.ds(tile + COL["ev_conv_b"], 1)], ALU.mult, ALU.add))
                            continue
                        a = v.scalar_tensor_tensor(out=conv[:, tile, :], in0=src, scalar=w, in1=conv[:, tile, :],
                                                   op0=ALU.mult, op1=ALU.add)
                        if n == CONV_TAPS - 1:
                            a.then_inc(sq_ready, 1)
                        else:
                            S.do(a)

            v.wait_ge(stat_done, 3)
            S.do(v.tensor_scalar(lnt[:, 0, :], px[0][:, 0:T], 1.0 / D, None, ALU.mult))
            S.sync()
            S.do(tt_(lnt[:, 1, :], lnt[:, 0, :], lnt[:, 0, :], ALU.mult))
            v.wait_ge(stat_done, 4)
            S.do(v.tensor_scalar(lnt[:, 2, :], px[1][:, 0:T], 1.0 / D, EPS5, ALU.mult, ALU.add))
            S.sync()
            v.tensor_tensor(lnt[:, 3, :], lnt[:, 2, :], lnt[:, 1, :], ALU.subtract).then_inc(var_ready, 1)
            v.wait_ge(sd_ready, 3)
            S.do(v.reciprocal(lnt[:, 4, :], lnt[:, 3, :]))
            S.sync()
            for s in range(KT + 1):
                if s < KT:
                    S.do(tt_(conv[:, s, :], conv[:, s, :], lnt[:, 0, :], ALU.subtract))
                if s >= 1:
                    k = s - 1
                    S.sync(S.n - (1 if s < KT else 0))
                    v.tensor_tensor(conv[:, k, :], conv[:, k, :], lnt[:, 4, :], ALU.mult).then_inc(ln_norm, 1)
            for k in range(KT):
                v.wait_ge(ln_silu, k + 1)
                v.wait_ge(ps_free[k % SLOTS], BASE["ga"] + k // SLOTS + 1)
                S.do(tt_(conv[:, k, :], conv[:, k, :], ga[:, k, :], ALU.mult))
                S.sync()
                S.do(v.tensor_copy(ya_hi[:, k, :], conv[:, k, :]))
                S.sync()
                v.tensor_tensor(ya_lo[:, k, :], conv[:, k, :], ya_hi[:, k, :].bitcast(F32), ALU.subtract) \
                 .then_inc(opnd, 1)

            for j in range(SLOTS):
                v.wait_ge(ps_free[j], BASE["gb"] + 2)
            for head in range(KT):
                b = head % 2
                uf = xpad[:, head, :, SCONV_LEFT:SCONV_LEFT + T]
                v.wait_ge(tanh_ready, 2 * head + 2)
                S.do(v.tensor_scalar(rec[:], tt[:, b], 1.0, None, ALU.add))
                for d in range(2):
                    i_d = iu[:, b, d, :].rearrange("p (s t) -> p s t", s=2)
                    S.do(tt_(i_d, i_d, uf, ALU.mult))
                S.sync(S.n - 2)
                S.do(v.reciprocal(rec[:], rec[:]))
                S.sync()
                S.do(v.tensor_scalar(aa[:], rec[:], 2.0, -1.0, ALU.mult, ALU.add))
                S.do(tt_(iu[:, b], iu[:, b], rec[:], ALU.mult))
                S.sync()
                v.wait_ge(root_ready, head + 1)
                S.do(v.scalar_tensor_tensor(out=iu[:, b], in0=rt[:, b], scalar=2.0, in1=iu[:, b], op0=ALU.mult,
                                            op1=ALU.mult))
                S.sync()
                S.do(v.tensor_tensor_scan(tt[:, b, 0, :], aa[:, 0, :], iu[:, b, 0, :], 0.0, ALU.mult, ALU.add))
                S.do(v.tensor_tensor_scan(tt[:, b, 1, T - 1::-1], aa[:, 1, T - 1::-1], iu[:, b, 1, T - 1::-1], 0.0,
                                          ALU.mult, ALU.add))
                S.sync()
                S.do(v.tensor_tensor_scan(tt[:, b, 1, 2 * T - 1:T - 1:-1], aa[:, 1, 2 * T - 1:T - 1:-1],
                                          iu[:, b, 1, 2 * T - 1:T - 1:-1], tt[:, b, 1, 0:1], ALU.mult, ALU.add))
                S.sync()
                S.do(tt_(tt[:, b, 0, T:], tt[:, b, 0, T:], tt[:, b, 1, T:], ALU.add))
                S.sync()
                v.tensor_tensor(gb[:, head, :], gb[:, head, :], tt[:, b, 0, T:], ALU.mult).then_inc(lru_free, 1)
                v.wait_ge(lru_free, head + 1)
                S.do(v.tensor_copy(yb_hi[:, head, :], gb[:, head, :]))
                S.sync()
                v.tensor_tensor(yb_lo[:, head, :], gb[:, head, :], yb_hi[:, head, :].bitcast(F32), ALU.subtract) \
                 .then_inc(opnd, 1)

            for s in range(MOD_SLOTS):
                v.wait_ge(modw_used[s], 2)
            S.do(tt_(gate0, mod[:, 0:KT], col("mod_b", 2 * KT, KT), ALU.add))
            S.sync()

            def add_to_x(name, gate):
                with v.Fori(0, ROUNDS_OF[name]) as i:
                    for j in range(SLOTS):
                        v.wait_ge(pe_done[j], i + (BASE[name] + 1))
                        v.wait_ge(ps_free[j], i + BASE[name])
                        xt = x[:, i * SLOTS + j, :]
                        v.scalar_tensor_tensor(out=xt, in0=ps[j][:, 0:T], scalar=gate[:, bass.ds(i * SLOTS + j, 1)],
                                               in1=xt, op0=ALU.mult, op1=ALU.add).then_inc(ps_free[j], 1)

            add_to_x("ya", gate0)
            for j in range(SLOTS):
                v.wait_ge(ps_free[j], BASE["ya"] + 2)
            add_to_x("yb", gate0)

            def affine_cols(scale, shift, g, b_name, b0, q0, src=mod):
                S.do(tt_(shift, src[:, q0:q0 + KT], col(b_name, b0, KT), ALU.add))
                S.do(tt_(scale, src[:, q0 + KT:q0 + 2 * KT], col(b_name, b0 + KT, KT), ALU.add))
                S.sync()
                S.do(v.scalar_tensor_tensor(out=scale, in0=scale, scalar=1.0, in1=g, op0=ALU.add, op1=ALU.mult))

            def mods_used(g):
                for s in range(MOD_SLOTS):
                    v.wait_ge(modw_used[s], g)

            def rstd(stat, bank, width, eps, t, dst, var_n):
                v.wait_ge(stat_done, stat)
                v.tensor_scalar(t, bank, 1.0 / width, eps, ALU.mult, ALU.add).then_inc(var_ready, 1)
                v.wait_ge(sd_ready, var_n)
                S.do(v.reciprocal(dst, t))
                S.sync()

            for g in range(2, 8):
                mod_tiles(g, 0)
            mods_used(8)
            affine_cols(sc1, shift1, col("norm_g", KT, KT), "mod_b", 3 * KT, KT)
            S.do(tt_(gate1, mod[:, 3 * KT:4 * KT], col("mod_b", 5 * KT, KT), ALU.add))
            for j in range(SLOTS):
                v.wait_ge(ps_free[j], BASE["od_u"])
            S.do(v.memset(opad[:, :, :, 0:8], 0.0))
            v.memset(opad[:, :, :, 8 + GRID_W:PW], 0.0).then_inc(pads_ready, 1)
            rstd(5, px[0][:, 0:T], D, EPS6, t1[:, 0, :], vr1[:], 4)
            modulate(KT, lambda k: x[:, k, :], vr1[:], lambda k: sc1[:, k:k + 1], lambda k: shift1[:, k:k + 1], t1,
                     lambda k: h1_hi[:, k, :], lambda k: h1_lo[:, k, :])
            v.wait_ge(opnd, OPND["h1"] + KT)

            def window(g, reach):
                src = opad[:, 4 * g:4 * g + 4, :, :].rearrange("p a r c -> p (a r) c")
                w = WINDOWS[g]
                steps = [2]
                while steps[-1] < w:
                    steps.append(2 * steps[-1])
                for n, size in enumerate(steps):
                    rest = sum(m // 4 for m in steps[n + 1:])
                    lo, hi_ = 8 - rest, 8 + GRID_W + rest
                    back, ahead = (1, 0) if size == 2 else (size // 4, size // 4)
                    S.do(tt_(win[n % 2][:, :, lo:hi_], src[:, :, lo - back:hi_ - back], src[:, :, lo + ahead:hi_ + ahead],
                             ALU.add))
                    S.sync()
                    src = win[n % 2]
                return src[:, :, 8:8 + GRID_W]

            def inner(g):
                return opad[:, 4 * g:4 * g + 4, :, 8:8 + GRID_W].rearrange("p a r c -> p (a r) c")

            pdv = pd[:].rearrange("p a (r c) -> p (a r) c", c=GRID_W)
            for g in range(len(WINDOWS)):
                for j in range(SLOTS):
                    v.wait_ge(ps_free[j], BASE["od_u"] + g + 1)
                if g:
                    v.wait_ge(opnd, OPND["d"] + g)
                mean = window(g, 0)
                c0 = CON["inv_count"] + g * GRID_W
                inv = con[:, c0:c0 + GRID_W].rearrange("p (a c) -> p a c", a=1).to_broadcast([P, 16, GRID_W])
                S.do(tt_(pdv, mean, inv, ALU.mult))
                S.sync()
                S.do(tt_(pdv, pdv, inner(g), ALU.subtract))
                S.sync()
                S.do(v.tensor_copy(d_hi[:, 4 * g:4 * g + 4, :], pd[:]))
                S.sync()
                v.tensor_tensor(d_lo[:, 4 * g:4 * g + 4, :], pd[:], d_hi[:, 4 * g:4 * g + 4, :].bitcast(F32),
                                ALU.subtract).then_inc(opnd, 1)
                for s in range(MOD_SLOTS):
                    t = (8 + g) * MOD_SLOTS + s
                    v.wait_ge(modw_in[s], 16 * (9 + g))
                    S.sync()
                    a = v.scalar_tensor_tensor(out=c_row[:, 0, :], in0=modw[s][:], scalar=1.0, in1=c_row[:, 2, :],
                                               op0=ALU.mult, op1=ALU.mult, accum_out=mod_c[:, t - 4 * KT:t - 4 * KT + 1])
                    S.do(a)
                    v.scalar_tensor_tensor(out=modw[s][:], in0=modw[s][:], scalar=1.0, in1=c_row[:, 1, :],
                                           op0=ALU.mult, op1=ALU.mult,
                                           accum_out=mod[:, t:t + 1]).then_inc(modw_used[s], 1)

            for i in S.loop(ROUNDS_OF["grp"], 2 * SLOTS):
                for j in range(SLOTS):
                    v.wait_ge(pe_done[j], i + (BASE["grp"] + 1))
                    v.wait_ge(ps_free[j], i + BASE["grp"])
                    t = i * 8 + 2 * j
                    yt = ytmp[:, j % 2]
                    for e in range(2):
                        a = v.scalar_tensor_tensor(
                            out=yt[:, e, :], in0=ps[j][:, e * T:(e + 1) * T],
                            scalar=cols[:, bass.ds(t + (COL["od_scale"] + e), 1)],
                            in1=og[:, t + e, :], op0=ALU.mult, op1=ALU.mult)
                        if e:
                            a.then_inc(ps_free[j], 1)
                        else:
                            S.do(a)
                    S.sync()
                    v.wait_ge(ps_free[j], i + (BASE["grp"] + 1))
                    S.do(v.tensor_copy(y_hi[:, bass.ds(t, 2), :], yt))
                    S.sync()
                    v.tensor_tensor(y_lo[:, bass.ds(t, 2), :], yt, y_hi[:, bass.ds(t, 2), :].bitcast(F32), ALU.subtract) \
                     .then_inc(opnd, 1)
            mods_used(12)
            affine_cols(sc2[0], sh2[0], col("g_mix_2", 0, KT), "b_mod_2", 0, 4 * KT)
            affine_cols(sc2[1], sh2[1], col("g_mix_2", 0, KT), "b_mod_2", 0, 0, mod_c)
            mod_tiles(12, 1)
            mod_tiles(13, 1)
            rstd(6, px[1][:, 0:T], D, EPS, vr[:, 0, :], vr[:, 3, :], 5)
            add_to_x("oda", gate1)
            v.wait_ge(ps_free[3], BASE["oda"] + 2)
            modulate(KT, lambda k: ctx2T[:, k, :], vr[:, 3, :], lambda k: sc2[1][:, k:k + 1],
                     lambda k: sh2[1][:, k:k + 1], t2, lambda k: h2_hi[:, 1, k, :], lambda k: h2_lo[:, 1, k, :])
            add_to_x("odb", gate1)

            rstd(7, px[0][:, 0:T], D, EPS6, vr[:, 1, :], vr[:, 0, :], 6)
            for k in range(KT):
                v.scalar_tensor_tensor(out=x[:, k, :], in0=x[:, k, :], scalar=col("final_g", k), in1=vr[:, 0, :],
                                       op0=ALU.mult, op1=ALU.mult).then_inc(x3_ready, 1)
            v.wait_ge(x3_ready, KT)
            rstd(8, px[2][:, 0:T], D, EPS, vr[:, 2, :], vr[:, 1, :], 7)
            modulate(KT, lambda k: x[:, k, :], vr[:, 1, :], lambda k: sc2[0][:, k:k + 1],
                     lambda k: sh2[0][:, k:k + 1], t2, lambda k: h2_hi[:, 0, k, :], lambda k: h2_lo[:, 0, k, :])
            for g in range(14, MOD_TILES // MOD_SLOTS):
                mod_tiles(g, 1)
            mods_used(MOD_TILES // MOD_SLOTS)
            S.do(tt_(gate2, mod[:, 6 * KT:7 * KT], col("b_mod_2", 2 * KT, KT), ALU.add))
            affine_cols(sc3, sh3, col("g_ffn_2", 0, KT), "b_mod_2", 3 * KT, 7 * KT)
            S.do(tt_(gate3, mod[:, 9 * KT:10 * KT], col("b_mod_2", 5 * KT, KT), ALU.add))

            n = 2 * HEADS
            g0, g1 = col("lb_gamma_2", 0, n), col("lb_gamma_2", n, n)
            S.do(tt_(lb_t[2], g0, g1, ALU.max))
            S.sync()
            S.do(tt_(lb_t[0], g0, lb_t[2], ALU.subtract))
            v.tensor_tensor(lb_t[1], g1, lb_t[2], ALU.subtract).then_inc(lb_in, 1)
            v.wait_ge(lb_ex, 2)
            S.do(tt_(lb_t[1], lb_t[0], lb_t[1], ALU.add))
            S.sync()
            S.do(v.reciprocal(lb_t[1], lb_t[1]))
            S.sync()
            S.do(tt_(lb, lb_t[0], lb_t[1], ALU.mult))
            S.sync()
            S.do(v.tensor_scalar(oml, lb, -1.0, 1.0, ALU.mult, ALU.add))
            S.sync()
            S.do(v.tensor_scalar(noml, oml, -1.0, None, ALU.mult))
            S.sync()
            for d in range(2):
                for h in range(HEADS):
                    v.wait_ge(ps_free[h], BASE["f"] + d + 1)
                    c = slice(HEADS * d + h, HEADS * d + h + 1)
                    S.do(v.tensor_scalar(Kk[:, d, h], Lg[:, d, h], noml[:, c], oml[:, c], ALU.mult, ALU.add))
                S.sync()
                for h in range(HEADS):
                    c = slice(HEADS * d + h, HEADS * d + h + 1)
                    a = v.tensor_scalar(Lg[:, d, h], Lg[:, d, h], oml[:, c], lb[:, c], ALU.mult, ALU.add)
                    if h == HEADS - 1:
                        a.then_inc(fk, 1)
                    else:
                        S.do(a)

            def scans(d):
                v.wait_ge(logf, d + 1)
                along = slice(None) if d == 0 else slice(None, None, -1)
                starts = con[:, CON["restart_b" if d else "restart_f"]:][:, 0:T]
                all_on = con[:, CON["ones"]:CON["ones"] + T]
                for h in range(HEADS):
                    for s, keep in ((0, starts), (1, all_on)):
                        S.do(v.tensor_tensor_scan(Lg[:, d, h, s, along], keep[:, along], Lg[:, d, h, s, along], 0.0,
                                                  ALU.mult, ALU.add))
                S.sync()

            def chunks(a):
                return a.rearrange("p h (c t) -> p h c t", t=CHUNK)

            def wide(c):
                return c.rearrange("p (h n a) -> p h n a", h=HEADS, a=1).to_broadcast([P, HEADS, CHUNKS, CHUNK])

            def direction(d):
                at_end = CHUNK - 1 if d == 0 else 0
                e0, g0_ = 9 * d, 4 + 10 * d
                Lx, Lc = chunks(Lg[:, d, :, 0, :]), Lg[:, d, :, 1, :]
                if d:
                    v.wait_ge(hg_pe, 14)
                S.do(v.tensor_copy(tots[:, HEADS * d:HEADS * d + HEADS], Lc[:, :, T - 1 if d == 0 else 0]))
                S.do(v.tensor_copy(bls.rearrange("p (h c) -> p h c", h=HEADS), Lx[:, :, :, at_end]))
                S.do(v.memset(sc[:], 0.0))
                S.sync()
                S.do(v.tensor_scalar(mids, bls, 0.5, None, ALU.mult))
                S.sync()
                v.tensor_tensor(chunks(tq[:]), Lx, wide(mids), ALU.subtract).then_inc(hx_dve, 1)
                v.wait_ge(hx_act, e0 + 8)
                v.tensor_tensor(Lx, wide(bls), Lx, ALU.subtract).then_inc(hx_dve, 1)
                Kc, Kx = Kk[:, d, :, 1, :], Kk[:, d, :, 0, :]
                v.tensor_tensor(Kc, Kc, Lc, ALU.mult).then_inc(hg_dve, 1)
                S.do(tt_(ki[:], ki[:], Kx, ALU.mult))
                for j in range(SLOTS):
                    v.wait_ge(ps_free[j], BASE["q"] + 1)
                v.tensor_tensor(qi[:], qi[:], q[:], ALU.mult).then_inc(hg_dve, 1)
                v.tensor_tensor(tq[:], tq[:], q[:], ALU.mult).then_inc(hg_dve, 1)
                v.wait_ge(hx_act, e0 + 9)
                v.tensor_tensor(Kx, Kx, Lg[:, d, :, 0, :], ALU.mult).then_inc(hg_dve, 1)
                order = (0, 1, 2, 3) if d == 0 else (3, 2, 1, 0)
                v.wait_ge(hg_pe, g0_ + 3)
                v.tensor_copy(St[:, order[0], :, :], px[0][:].rearrange("p (h e) -> p h e", h=HEADS)).then_inc(hg_dve, 1)
                for n in range(3):
                    v.wait_ge(hg_pe, g0_ + 6 + n)
                    if n:
                        S.sync()
                    v.wait_ge(hg_dve, 9 * d + 5 + n)
                    for h in range(HEADS):
                        c = HEADS * 0 + h * CHUNKS + order[n]
                        a = v.scalar_tensor_tensor(out=St[:, order[n + 1], h, :], in0=St[:, order[n], h, :],
                                                   scalar=dec[:, c:c + 1], in1=px[n % 2][:, h * P:(h + 1) * P],
                                                   op0=ALU.mult, op1=ALU.add)
                        if h == HEADS - 1:
                            a.then_inc(hg_dve, 1)
                        else:
                            S.do(a)
                v.wait_ge(hg_pe, g0_ + 9)
                v.wait_ge(in_sgu, 48)
                mask = tri[:, d:d + 1, :].to_broadcast([P, HEADS, P])
                S.do(v.copy_predicated(sc[:, 0:HEADS, :], mask, px[0][:].rearrange("p (r t) -> p r t", t=P)))
                v.copy_predicated(sc[:, HEADS:, :], mask, px[1][:].rearrange("p (r t) -> p r t", t=P)) \
                 .then_inc(hg_dve, 1)

            scans(0)
            scans(1)
            direction(0)
            direction(1)

            def split(hi, lo, src):
                S.do(v.tensor_copy(hi, src))
                S.sync()
                v.tensor_tensor(lo, src, hi.bitcast(F32), ALU.subtract).then_inc(opnd, 1)

            v.wait_ge(sg_pe, 1)
            S.do(v.tensor_scalar(ors[:, 0:2, :], px[0][:].rearrange("p (h t) -> p h t", h=2), 1.0 / P, EPS, ALU.mult,
                                 ALU.add))
            S.sync()
            v.wait_ge(sg_pe, 2)
            v.tensor_scalar(ors[:, 2:4, :], px[1][:].rearrange("p (h t) -> p h t", h=2), 1.0 / P, EPS, ALU.mult,
                            ALU.add).then_inc(var_ready, 1)
            v.wait_ge(sd_ready, 8)
            S.do(v.reciprocal(ors[:], ors[:]))
            S.sync()
            for n in range(2):
                S.do(tt_(o1[:, 2 * n:2 * n + 2, :], px[2 + n][:].rearrange("p (h t) -> p h t", h=2),
                         ors[:, 2 * n:2 * n + 2, :], ALU.mult))
            S.sync()
            for j in range(SLOTS):
                v.wait_ge(ps_free[j], BASE["uvo"] + 3)
            S.do(v.scalar_tensor_tensor(out=o1[:], in0=o1[:], scalar=col("g_norm_a_2"), in1=og2[:], op0=ALU.mult,
                                        op1=ALU.mult))
            S.sync()
            split(oa_hi[:], oa_lo[:], o1[:])

            v.wait_ge(sg_pe, 3)
            S.do(v.tensor_scalar(lnv[:, 0, :], px[0][:, 0:T], 1.0 / (HEADS * P), None, ALU.mult))
            S.sync()
            S.do(tt_(lnv[:, 1, :], lnv[:, 0, :], lnv[:, 0, :], ALU.mult))
            v.wait_ge(sg_pe, 4)
            S.do(v.tensor_scalar(lnv[:, 2, :], px[1][:, 0:T], 1.0 / (HEADS * P), EPS, ALU.mult, ALU.add))
            S.sync()
            v.tensor_tensor(lnv[:, 3, :], lnv[:, 2, :], lnv[:, 1, :], ALU.subtract).then_inc(var_ready, 1)
            v.wait_ge(sd_ready, 9)
            S.do(v.reciprocal(lnv[:, 1, :], lnv[:, 3, :]))
            S.sync()

            def by_token(a):
                return a.rearrange("p (n t) -> p n t", n=1).to_broadcast([P, HEADS, T])

            S.do(tt_(vn[:], v2[:], by_token(lnv[:, 0, :]), ALU.subtract))
            S.sync()
            S.do(tt_(vn[:], vn[:], by_token(lnv[:, 1, :]), ALU.mult))
            S.sync()
            for g in range(HEADS):
                a = v.tensor_scalar(vn[:, g, :], vn[:, g, :], col("ln_v_g_2", g), col("ln_v_b_2", g), ALU.mult, ALU.add)
                if g == HEADS - 1:
                    a.then_inc(sg_dve, 1)
                else:
                    S.do(a)
            v.wait_ge(sg_pe, 7)
            for n in range(2):
                S.do(tt_(ob[:, 2 * n:2 * n + 2, :], px[n][:].rearrange("p (g t) -> p g t", g=2),
                         u2[:, 2 * n:2 * n + 2, :], ALU.mult))
            S.sync()
            split(ob_hi[:], ob_lo[:], ob[:])

            for i in S.loop(ROUNDS_OF["pab"], 4):
                for e in range(2):
                    t = bass.ds(i * 4 + 2 * e, 2)
                    for part, gate in ((0, ga2), (1, gb2)):
                        j = 2 * e + part
                        v.wait_ge(pe_done[j], i + (BASE["pab"] + 1))
                        v.wait_ge(ps_free[j], i + BASE["pab"])
                        v.tensor_tensor(mt[:, e, part], ps[j][:].rearrange("p (n t) -> p n t", n=2), gate[:, t, :],
                                        ALU.mult).then_inc(ps_free[j], 1)
                    v.wait_ge(ps_free[2 * e], i + (BASE["pab"] + 1))
                    v.wait_ge(ps_free[2 * e + 1], i + (BASE["pab"] + 1))
                    S.do(tt_(mt[:, e, 0], mt[:, e, 0], mt[:, e, 1], ALU.add))
                    S.sync()
                    S.do(v.tensor_copy(m_hi[:, t, :], mt[:, e, 0]))
                    S.sync()
                    v.tensor_tensor(m_lo[:, t, :], mt[:, e, 0], m_hi[:, t, :].bitcast(F32), ALU.subtract) \
                     .then_inc(opnd, 1)
            add_to_x("wo", gate2)
            rstd(9, px[0][:, 0:T], D, EPS, v4[:, 0, :], v4[:, 1, :], 10)
            modulate(KT, lambda k: x[:, k, :], v4[:, 1, :], lambda k: sc3[:, k:k + 1], lambda k: sh3[:, k:k + 1],
                     t4, lambda k: h3_hi[:, k, :], lambda k: h3_lo[:, k, :])
            for i in S.loop(ROUNDS_OF["up"], 2):
                for e in range(2):
                    t = i * 2 + e
                    v.wait_ge(ps_free[2 * e], i + (BASE["up"] + 1))
                    v.wait_ge(pe_done[2 * e + 1], i + (BASE["up"] + 1))
                    v.wait_ge(ps_free[2 * e + 1], i + BASE["up"])
                    v.tensor_tensor(ff[:, e, :], ps[2 * e + 1][:, 0:T], sa[:, e, :], ALU.mult) \
                     .then_inc(ps_free[2 * e + 1], 1)
                    v.wait_ge(ps_free[2 * e + 1], i + (BASE["up"] + 1))
                    S.do(v.tensor_copy(ff_hi[:, t, :], ff[:, e, :]))
                    S.sync()
                    v.tensor_tensor(ff_lo[:, t, :], ff[:, e, :], ff_hi[:, t, :].bitcast(F32), ALU.subtract) \
                     .then_inc(opnd, 1)
            for name in ("dna", "dnb", "dnc"):
                add_to_x(name, gate3)
            rstd(10, px[0][:, 0:T], D, EPS, v4[:, 0, :], v4[:, 1, :], 11)
            for k in range(KT):
                v.scalar_tensor_tensor(out=x[:, k, :], in0=x[:, k, :], scalar=col("g_final_2", k), in1=v4[:, 1, :],
                                       op0=ALU.mult, op1=ALU.mult).then_inc(stored, 1)


def halves(w, tiles, k0=0, n=8):
    w = w[k0 * P:(k0 + n) * P]
    b = w.reshape(n, P, w.shape[1] // P, P)[:, :, list(tiles), :].transpose(2, 1, 0, 3)
    if n < 8:
        b = np.concatenate([b, np.zeros((b.shape[0], P, 8 - n, P), b.dtype)], axis=2)
    return b


def pairs(w):
    return w.reshape(4, P, w.shape[1] // (2 * P), 2, P).transpose(2, 1, 3, 0, 4).reshape(-1, P, 8, P)


def weight_stream(a):
    w = a["ev_w_in"][0]
    parts = [halves(w, range(24, 32))]
    va, vg = halves(w, range(0, 8)), halves(w, range(8, 16))
    parts.append(np.stack([va, vg], axis=1).reshape(16, P, 8, P))
    parts += [halves(w, range(16, 24)), halves(w, range(32, 40))]
    g = np.stack([a["ev_w_r"][0], a["ev_w_i"][0]], axis=1)
    parts.append(g.transpose(2, 0, 1, 3, 4).reshape(4, 8, P, P).transpose(0, 2, 1, 3))
    w = a["ev_w_out"][0]
    parts += [halves(w, range(8), 0), halves(w, range(8), 8)]
    parts.append(halves(a["od_w_in"][0], range(32)))
    parts.append(np.concatenate([pairs(m) for m in a["od_w_grp"][0]]))
    w = a["od_w_out"][0]
    parts += [halves(w, range(8), 0), halves(w, range(8), 8)]
    w = a["w_in_2"][0]
    parts.append(halves(w, range(0, 16)))
    parts.append(halves(w, range(20, 28)))
    parts.append(halves(w, range(16, 20)))
    parts.append(halves(w, range(28, 44)))
    pab = np.stack([pairs(a["w_pa_2"][0]), pairs(a["w_pb_2"][0])], axis=1)
    parts.append(pab.reshape(8, P, 8, P))
    parts.append(halves(a["w_o_2"][0], range(8)))
    w = a["w_up_2"][0]
    up = np.stack([halves(w, range(FT)), halves(w, range(FT, 2 * FT))], axis=1)
    parts.append(up.reshape(2 * FT, P, 8, P))
    w = a["w_down_2"][0]
    parts += [halves(w, range(8), 0), halves(w, range(8), 8), halves(w, range(8), 16, 6)]
    return np.ascontiguousarray(np.concatenate(parts)).reshape(-1, P, 8, P)


def kernel(**inputs):
    import concourse.bacc as bacc
    from concourse.bass_utils import run_bass_kernel_spmd

    a = {n: np.asarray(v) for n, v in inputs.items()}

    def feature_major(v):
        return np.ascontiguousarray(v.reshape(T, KT, P).transpose(2, 1, 0))

    s, t = np.arange(P)[:, None], np.arange(P)[None, :]
    same = s // CHUNK == t // CHUNK
    tt = np.arange(T)
    count = []
    for w in WINDOWS:
        g = np.arange(GRID_W)
        count.append(np.minimum(g + w // 2, GRID_W) - np.maximum(g - w // 2, 0))
    rows = [np.eye(P), np.ones((P, T)), np.tile(tt % CHUNK != 0, (P, 1)), np.tile(tt % CHUNK != CHUNK - 1, (P, 1)),
            np.tile(1.0 / np.concatenate(count), (P, 1))]
    mod_w = np.concatenate([a["mod_w"][0][:, 2 * D:], a["mod_w"][1], a["w_mod_2"][0]], axis=1)
    arrays = {
        "c_cols": np.stack([a["c"][0], a["c_ctx"]], axis=1).reshape(KT, P, 2).transpose(1, 0, 2).reshape(P, 2 * KT),
        "c_rows": np.stack([a["c"][0], a["c_2"][0], a["c_ctx_2"]]),
        "mod0_w": halves(a["mod_w"][0], range(16)),
        "mod_w": mod_w.T.reshape(MOD_TILES, P, D),
        "ctxT": feature_major(a["ctx"][0]),
        "xT": feature_major(a["x"][0]),
        "cols": np.concatenate([a[n].reshape(-1, P) for n, _ in PARAMS]).T,
        "con": np.concatenate([r.astype(np.float32) for r in rows], axis=1),
        "tri": np.stack([same & (s <= t), same & (s >= t)], axis=1).astype(np.int32),
        "ctx2T": feature_major(a["ctx_2"][0]),
        "wsT": a["w_s_2"][0].transpose(2, 0, 1),
        "b_s": a["b_s_2"].reshape(1, HEADS * P),
        "stream": weight_stream(a),
    }
    arrays = {n: np.ascontiguousarray(v) for n, v in arrays.items()}
    nc = bacc.Bacc("TRN2", target_bir_lowering=False, num_devices=1)
    ins = {n: nc.dram_tensor(f"in_{n}", v.shape, mybir.dt.from_np(v.dtype), kind="ExternalInput").ap()
           for n, v in arrays.items()}
    out = nc.dram_tensor("out_xT", (P, KT, T), F32, kind="ExternalOutput").ap()
    build(nc, ins, out)
    r = run_bass_kernel_spmd(nc, [{f"in_{n}": v for n, v in arrays.items()}], core_ids=[0])
    got = r.results[0]["out_xT"]
    return got.transpose(2, 1, 0).reshape(1, T, D)
```

```python
from contextlib import ExitStack

import numpy as np
import concourse.bass as bass
from concourse import mybir

F32 = mybir.dt.float32
F32R = mybir.dt.float32r
I32 = mybir.dt.int32
ALU = mybir.AluOpType
ACT = mybir.ActivationFunctionType

P = 128
D = 1024
T = 256
KT = D // P
SLOTS = 4
HALF = 8 * P
EPS6, EPS5 = 1e-6, 1e-5
EPS = 1e-6
GRID_W = 64
CONV_TAPS = 31
CONV_LEFT = CONV_TAPS // 2
SCONV_TAPS = 4
SCONV_LEFT = 2
WINDOWS = (2, 4, 8, 16)
HEADS = 4
CHUNK = 64
CHUNKS = T // CHUNK
FF = 2816
FT = FF // P

PHASES = [
    ("xb", 2), ("vavg", 4), ("ga", 2), ("g0", 1), ("cv", 4), ("g1", 1), ("g2", 1), ("ya", 2), ("yb", 2),
    ("od_u", 4), ("od_g", 4), ("grp", 2), ("oda", 2), ("odb", 2),
    ("f", 2), ("i", 1), ("q", 1), ("uvo", 3), ("ga2", 2), ("gb2", 2), ("pab", 2), ("wo", 2), ("up", 11),
    ("dna", 2), ("dnb", 2), ("dnc", 2),
]
GATE_SLOT = [("g0", 0), ("g1", 0), ("g2", 2), ("g2", 3)]
GB_SLOT = [("g1", 1), ("g1", 2), ("g1", 3), ("g2", 0), ("g2", 1), ("g0", 1), ("g0", 2), ("g0", 3)]
BASE, ROUNDS_OF = {}, {}
_n = 0
for _name, _rounds in PHASES:
    BASE[_name], ROUNDS_OF[_name] = _n, _rounds
    _n += _rounds
ROUNDS = _n

MOD_TILES = KT + 3 * KT + 6 * KT
MOD_SLOTS = 4

PARAMS = [
    ("norm_g", 16), ("mod_b", 48), ("ev_conv_w", 31 * 8), ("ev_conv_b", 8), ("ev_ln_g", 8), ("ev_ln_b", 8),
    ("ev_sconv_w", 32), ("ev_sconv_b", 8), ("ev_b_r", 16), ("ev_b_i", 16), ("ev_lam", 16), ("od_scale", 16),
    ("final_g", 8), ("b_mod_2", 48), ("g_mix_2", 8), ("g_ffn_2", 8), ("lb_gamma_2", 16), ("g_norm_a_2", 1),
    ("ln_v_g_2", 4), ("ln_v_b_2", 4), ("g_final_2", 8),
]
COL = {}
_n = 0
for _name, _cols in PARAMS:
    COL[_name] = _n
    _n += _cols
NCOLS = _n

CONSTS = [("ident", P), ("ones", T), ("restart_f", T), ("restart_b", T), ("inv_count", len(WINDOWS) * GRID_W)]
CON = {}
_n = 0
for _name, _cols in CONSTS:
    CON[_name] = _n
    _n += _cols
NCONS = _n


class Steps:

    def __init__(self, eng, sem):
        self.eng, self.sem, self.n = eng, sem, 0

    def do(self, ins):
        ins.then_inc(self.sem, 1)
        self.n = self.n + 1
        return self.n

    def sync(self, n=None):
        self.eng.wait_ge(self.sem, self.n if n is None else n)

    def loop(self, count, per_round):
        start = self.n
        with self.eng.Fori(0, count) as i:
            self.n = i * per_round + start
            yield i
        self.n = start + count * per_round


def build(nc, ins, out):
    with ExitStack() as ctx:
        base = nc.sbuf_base + (-nc.sbuf_base) % 32

        def at(name, kib, shape, dt=F32):
            return nc.alloc_sbuf_tensor_at(name, [P] + shape, dt, offset=base + int(kib * 1024))

        def sem(name):
            return ctx.enter_context(nc.semaphore(name))

        raw = [at(f"raw{j}", 4 * j, [8, P]) for j in range(SLOTS)]
        w_hi = [at(f"w_hi{j}", 16 + 4 * j, [8, P], F32R) for j in range(SLOTS)]
        w_lo = [at(f"w_lo{j}", 32 + 4 * j, [8, P], F32R) for j in range(SLOTS)]
        modw = [at(f"modw{j}", 48 + 4 * j, [D]) for j in range(MOD_SLOTS)]
        c_row = at("c_row", 64, [3, D])
        x = at("x", 76, [KT, T])
        cols = at("cols", 84, [NCOLS])
        con = at("con", 86.5, [NCONS])
        mod = at("mod", 91, [MOD_TILES])
        mod_c = at("mod_c", 91.375, [2 * KT])
        mod0 = at("mod0", 91.5, [2 * KT, 2])
        small = at("small", 91.75, [448])
        W = 94

        ident = con[:, CON["ident"]:CON["ident"] + P]
        ones = con[:, CON["ones"]:CON["ones"] + P]

        def col(name, n=0, k=1):
            return cols[:, COL[name] + n:COL[name] + n + k]

        used = [0]

        def columns(n):
            used[0] += n
            assert used[0] <= 448
            return small[:, used[0] - n:used[0]]

        m0 = at("m0", W, [KT, 2 * D])
        mrow = at("mrow", W + 64, [2 * D])
        h_hi = at("h_hi", W, [2, KT, T], F32R)
        h_lo = at("h_lo", W + 16, [2, KT, T], F32R)
        u_hi = at("u_hi", W + 32, [KT, 2, T], F32R)
        u_lo = at("u_lo", W + 48, [KT, 2, T], F32R)
        XW = T + SCONV_TAPS
        xpad = at("xpad", W + 64, [KT, 2, XW])
        UW = T + CONV_TAPS + 1
        CV = KT // 2
        upad = at("upad", W + 80.25, [CV, UW])
        cv_hi = at("cv_hi", W + 84.75, [CV, UW], F32R)
        cv_lo = at("cv_lo", W + 105.25, [CV, UW], F32R)
        va_in = at("va_in", W + 105.25, [CV, UW])
        conv = at("conv", W + 89.25, [KT, T])
        ga = at("ga", W + 97.25, [KT, T])
        gb = at("gb", W + 105.25, [KT, T])
        ctxT = at("ctxT", W + 97.25, [KT, T])
        sq0 = at("sq0", W + 105.25, [KT, T])
        t0 = at("t0", W + 80.25, [8, T])
        stmp = at("stmp", W + 97.25, [4, 2, T])
        ya_hi = at("ya_hi", W + 80.25, [KT, T], F32R)
        ya_lo = at("ya_lo", W + 89.25, [KT, T], F32R)
        yb_hi = at("yb_hi", W + 97.25, [KT, T], F32R)
        yb_lo = at("yb_lo", W + 105.25, [KT, T], F32R)
        lnsq = at("lnsq", 48, [KT, T])
        lnt = at("lnt", 56, [8, T])
        LB = 4
        PAIR_BUF = (0, 0, 2, 0)
        lr = at("lr", W, [LB, 2, 2 * T])
        li = at("li", W + 16, [LB, 2, 2 * T])
        la = at("la", W + 32, [2, KT, 2 * T])
        asq = at("asq", 72, [2, 2 * T])

        sq1 = at("sq1", W, [KT, T])
        h1_hi = at("h1_hi", W + 8, [KT, T], F32R)
        h1_lo = at("h1_lo", W + 16, [KT, T], F32R)
        t1 = at("t1", W + 24, [8, T])
        PW = GRID_W + 16
        ROWS = T // GRID_W
        opad = at("opad", W + 32, [16, ROWS, PW])
        og = at("og", W + 52, [16, T])
        d_hi = at("d_hi", W + 68, [16, T], F32R)
        d_lo = at("d_lo", W + 84, [16, T], F32R)
        win = [at("win0", W, [16, PW]), at("win1", W + 24, [16, PW])]
        pd = at("pd", W + 100, [4, T])
        vr1 = at("vr1", W + 100, [T])
        ytmp = at("ytmp", W + 104, [2, 2, T])
        y_hi = at("y_hi", W + 8, [16, T], F32R)
        y_lo = at("y_lo", W + 32, [16, T], F32R)

        ctx2T = at("ctx2T", W + 24, [KT, T])
        sqc = at("sqc", W, [KT, T])
        sq2 = at("sq2", W + 48, [KT, T])
        t2 = at("t2", W + 56, [8, T])
        vr = at("vr", W + 64, [4, T])
        h2_hi = at("h2_hi", W + 68, [2, KT, T], F32R)
        h2_lo = at("h2_lo", W + 84, [2, KT, T], F32R)
        Lg = at("Lg", W, [2, HEADS, 2, T])
        Kk = at("Kk", W + 16, [2, HEADS, 2, T])
        V = at("V", W + 32, [HEADS, 2, T])
        q = at("q", W + 40, [HEADS, T])
        og2 = at("og2", W + 44, [HEADS, T])
        u2 = at("u2", W + 48, [HEADS, T])
        v2 = at("v2", W + 52, [HEADS, T])
        tq = at("tq", W + 56, [HEADS, T])
        qi = at("qi", W + 60, [HEADS, T])
        ki = at("ki", W + 64, [HEADS, T])
        St = at("St", W + 76, [CHUNKS, HEADS, P])
        vtok = at("vtok", W + 92, [2, 2, HEADS, P])
        kdT = at("kdT", W + 100, [HEADS, 2, P])
        sc = at("sc", W + 104, [HEADS * 2, P])
        wsT = at("wsT", W + 108, [HEADS, P])
        bsr = at("bsr", W + 110, [HEADS * P])
        tri = at("tri", W + 112, [2, P], I32)
        ga2 = at("ga2", 48, [KT, T])
        gb2 = at("gb2", 56, [KT, T])
        osq = at("osq", W + 56, [HEADS, T])
        ors = at("ors", W + 60, [HEADS, T])
        o1 = at("o1", W + 64, [HEADS, T])
        vn = at("vn", W + 32, [HEADS, T])
        vsq = at("vsq", W + 36, [HEADS, T])
        lnv = at("lnv", W + 4, [4, T])
        vt = at("vt", W, [2, HEADS, P])
        ob = at("ob", W + 16, [HEADS, T])
        oa_hi, oa_lo = at("oa_hi", W, [HEADS, T], F32R), at("oa_lo", W + 4, [HEADS, T], F32R)
        ob_hi, ob_lo = at("ob_hi", W + 20, [HEADS, T], F32R), at("ob_lo", W + 36, [HEADS, T], F32R)
        m_hi, m_lo = at("m_hi", W + 68, [KT, T], F32R), at("m_lo", W + 76, [KT, T], F32R)
        mt = at("mt", W + 84, [2, 2, 2, T])

        sq4 = at("sq4", W, [KT, T])
        t4 = at("t4", W + 8, [8, T])
        h3_hi, h3_lo = at("h3_hi", W + 32, [KT, T], F32R), at("h3_lo", W + 40, [KT, T], F32R)
        ff_hi, ff_lo = at("ff_hi", W + 48, [FT, T], F32R), at("ff_lo", W + 70, [FT, T], F32R)
        sa = at("sa", W + 92, [2, T])
        ff = at("ff", W + 94, [2, T])
        v4 = at("v4", W + 98, [2, T])
        sq5 = at("sq5", W, [KT, T])

        ps = [ctx.enter_context(nc.psum_tensor(f"ps{j}", [P, 2 * T], F32)) for j in range(SLOTS)]
        px = [ctx.enter_context(nc.psum_tensor(f"px{j}", [P, 2 * T], F32)) for j in range(4)]

        raw_in = [sem(f"raw_in{j}") for j in range(SLOTS)]
        mod0_in = [sem(f"mod0_in{n}") for n in range(KT)]
        hi_ready = [sem(f"hi_ready{j}") for j in range(SLOTS)]
        lo_ready = [sem(f"lo_ready{j}") for j in range(SLOTS)]
        pe_done = [sem(f"pe_done{j}") for j in range(SLOTS)]
        ps_free = [sem(f"ps_free{j}") for j in range(SLOTS)]
        modw_in = [sem(f"modw_in{j}") for j in range(MOD_SLOTS)]
        modw_used = [sem(f"modw_used{j}") for j in range(MOD_SLOTS)]
        in_cc, in_con, in_x, in_ctx, in_crow = (sem(n) for n in ("in_cc", "in_con", "in_x", "in_ctx", "in_crow"))
        in_crow2 = sem("in_crow2")
        xn_ready = sem("xn_ready")
        modc_ready = sem("modc_ready")
        pre_ready = sem("pre_ready")
        act_hi = sem("act_hi")
        h0_hi = sem("h0_hi")
        conv_done = sem("conv_done")
        cc_ready = sem("cc_ready")
        crow_ready = sem("crow_ready")
        sq_ready = sem("sq_ready")
        stat_done = sem("stat_done")
        var_ready = sem("var_ready")
        sd_ready = sem("sd_ready")
        opnd = sem("opnd")
        mod0_rows = sem("mod0_rows")
        mod0_out = sem("mod0_out")
        mod0_done = sem("mod0_done")
        softplus_in = sem("softplus_in")
        softplus_ex = sem("softplus_ex")
        lru_cols = sem("lru_cols")
        gates_pe = sem("gates_pe")
        gates_out = sem("gates_out")
        exp_ready = sem("exp_ready")
        tanh_ready = sem("tanh_ready")
        prod_ready = sem("prod_ready")
        root_ready = sem("root_ready")
        lru_free = sem("lru_free")
        pads_ready = sem("pads_ready")
        in_ctx2, in_sgu = sem("in_ctx2"), sem("in_sgu")
        lb_in, lb_ex = sem("lb_in"), sem("lb_ex")
        fk = sem("fk")
        logf = sem("logf")
        hx_dve, hx_act = sem("hx_dve"), sem("hx_act")
        hg_dve, hg_act, hg_pe = sem("hg_dve"), sem("hg_act"), sem("hg_pe")
        sg_dve, sg_act, sg_pe = sem("sg_dve"), sem("sg_act"), sem("sg_pe")
        silu_ready = sem("silu_ready")
        stored = sem("stored")
        x3_ready = sem("x3_ready")
        ln_sq, ln_norm, ln_silu = sem("ln_sq"), sem("ln_norm"), sem("ln_silu")
        dve_step = sem("dve_step")
        act_step = sem("act_step")
        out_done = sem("out_done")

        modA = [columns(KT), columns(KT)]
        modS = [columns(KT), columns(KT)]
        gate0 = columns(KT)
        sc2 = [columns(KT), columns(KT)]
        sh2 = [columns(KT), columns(KT)]
        gate2, sc3, sh3, gate3 = columns(KT), columns(KT), columns(KT), columns(KT)
        tots, bls, mids, dec = columns(8), columns(16), columns(16), columns(16)
        lru_z, lru_nz = columns(2 * KT), columns(2 * KT)
        lam_t = [columns(2 * KT) for _ in range(4)]
        ccs = columns(2 * KT)
        warm = columns(1)
        sc1, gate1 = columns(KT), columns(KT)
        shift1 = columns(KT)
        lb_t = [columns(2 * HEADS) for _ in range(3)]
        lb, oml, noml = (columns(2 * HEADS) for _ in range(3))

        block = ctx.enter_context(nc.Block())

        OPND, n = {}, 0
        for name, tiles in (("h0", 16), ("u", 8), ("cv", 4), ("ya", 8), ("yb", 8), ("h1", 8), ("d", 4), ("y", 8),
                            ("hc2", 8), ("h2", 8), ("ob", 1), ("oa", 1), ("m", 4), ("h3", 8), ("ff", FT)):
            OPND[name] = n
            n += tiles

        @block.sync
        def _(sp):
            sp.dma_start(ccs, ins["c_cols"]).then_inc(in_cc, 16)
            sp.dma_start(x[:], ins["xT"]).then_inc(in_x, 16)
            sp.dma_start(ctxT[:], ins["ctxT"]).then_inc(in_ctx, 16)
            sp.dma_start(con[:], ins["con"]).then_inc(in_con, 16)
            sp.dma_start(cols[:], ins["cols"]).then_inc(in_con, 16)
            for k in range(KT):
                sp.dma_start(m0[:, k, :], ins["mod0_w"][k]).then_inc(mod0_in[k], 16)
            for j in range(SLOTS):
                sp.dma_start(raw[j][:], ins["stream"][j]).then_inc(raw_in[j], 16)
            for n in range(2):
                sp.dma_start(c_row[:, n, :], ins["c_rows"][n:n + 1, :].partition_broadcast(P)).then_inc(in_crow, 16)

            def mod_group(g):
                for s in range(MOD_SLOTS):
                    if g:
                        sp.wait_ge(modw_used[s], g)
                    sp.dma_start(modw[s][:], ins["mod_w"][g * MOD_SLOTS + s]).then_inc(modw_in[s], 16)

            def rounds(first, end):
                with sp.Fori(first, end) as r:
                    for j in range(SLOTS):
                        sp.wait_ge(lo_ready[j], r)
                        sp.dma_start(raw[j][:], ins["stream"][r * SLOTS + j]).then_inc(raw_in[j], 16)

            def round_and_mod(r, g):
                for j in range(SLOTS):
                    sp.wait_ge(lo_ready[j], r)
                    sp.dma_start(raw[j][:], ins["stream"][r * SLOTS + j]).then_inc(raw_in[j], 16)
                    sp.wait_ge(modw_used[j], g)
                    sp.dma_start(modw[j][:], ins["mod_w"][g * MOD_SLOTS + j]).then_inc(modw_in[j], 16)

            mod_group(0)
            rounds(1, 2)
            round_and_mod(2, 1)
            round_and_mod(3, 2)
            rounds(4, 7)
            round_and_mod(7, 3)
            round_and_mod(8, 4)
            round_and_mod(9, 5)
            rounds(10, 11)
            round_and_mod(11, 6)
            round_and_mod(12, 7)
            rounds(13, BASE["od_u"])
            sp.wait_ge(opnd, OPND["yb"] + KT)
            sp.dma_start(c_row[:, 2, :], ins["c_rows"][2:3, :].partition_broadcast(P)).then_inc(in_crow2, 16)
            mod_group(8)
            rounds(BASE["od_u"], BASE["od_u"] + 4)
            round_and_mod(BASE["od_u"] + 4, 9)
            rounds(BASE["od_u"] + 5, BASE["od_u"] + 6)
            round_and_mod(BASE["od_u"] + 6, 10)
            rounds(BASE["od_u"] + 7, BASE["grp"])
            round_and_mod(BASE["grp"], 11)
            rounds(BASE["grp"] + 1, BASE["oda"])
            sp.wait_ge(opnd, OPND["d"] + 4)
            sp.dma_start(ctx2T[:], ins["ctx2T"]).then_inc(in_ctx2, 16)
            rounds(BASE["oda"], BASE["odb"])
            round_and_mod(BASE["odb"], 12)
            rounds(BASE["odb"] + 1, BASE["i"])
            for g in (13, 14, 15):
                mod_group(g)
            rounds(BASE["i"], BASE["q"])
            mod_group(16)
            sp.wait_ge(ps_free[3], BASE["f"])
            sp.dma_start(wsT[:], ins["wsT"]).then_inc(in_sgu, 16)
            sp.dma_start(bsr[0:1, :], ins["b_s"]).then_inc(in_sgu, 16)
            sp.dma_start(tri[:], ins["tri"]).then_inc(in_sgu, 16)
            rounds(BASE["q"], BASE["uvo"])
            mod_group(17)
            rounds(BASE["uvo"], BASE["up"])
            sp.wait_ge(opnd, OPND["m"] + 4)
            mod_group(18)
            rounds(BASE["up"], BASE["up"] + 2)
            mod_group(19)
            rounds(BASE["up"] + 2, ROUNDS)
            for k in range(KT):
                sp.wait_ge(stored, k + 1)
                sp.dma_start(out[:, k, :], x[:, k, :]).then_inc(out_done, 16)
            sp.wait_ge(out_done, 16 * KT)

        @block.gpsimd
        def _(pool):
            with pool.Fori(0, ROUNDS) as r:
                for j in range(SLOTS):
                    pool.wait_ge(hi_ready[j], r + 1)
                    pool.tensor_tensor(w_lo[j][:], raw[j][:], w_hi[j][:].bitcast(F32),
                                       ALU.subtract).then_inc(lo_ready[j], 1)

        @block.tensor
        def _(pe):
            def first_modulation():
                for k in range(KT):
                    pe.wait_ge(mod0_in[k], 16)
                    for n in range(SLOTS):
                        last = pe.matmul(ps[n][0:2, :], ccs[:, 2 * k:2 * k + 2], m0[:, k, n * 2 * T:(n + 1) * 2 * T],
                                         start=(k == 0), stop=(k == KT - 1))
                        if k == KT - 1:
                            last.then_inc(mod0_rows, 1)
                for n in range(2 * KT):
                    pe.wait_ge(mod0_out, n // SLOTS + 1)
                    last = pe.transpose(px[3][:, 2 * n:2 * n + 2], mrow[0:2, n * P:(n + 1) * P], ident[0:2, 0:2])
                last.then_inc(mod0_done, 1)

            def stats(bank, squares, ready, signal=sq_ready, tiles=KT):
                for k in range(tiles):
                    pe.wait_ge(signal, ready + k + 1)
                    last = pe.matmul(bank[:, 0:T], ones, squares(k), start=(k == 0),
                                     stop=(k == tiles - 1))
                last.then_inc(stat_done, 1)

            def half(name, i, j, hi, lo, width, opnds=None, tiles=KT, step=1, first=False):
                pe.wait_ge(lo_ready[j], i + (BASE[name] + 1))
                if not first:
                    pe.wait_ge(ps_free[j], i + BASE[name])
                for k in range(tiles):
                    if j == 0 and opnds is not None:
                        pe.wait_ge(opnd, opnds + step * (k + 1))
                    pe.matmul(ps[j][:, 0:width], w_hi[j][:, k, :], hi(k), start=(k == 0), stop=False)
                    pe.matmul(ps[j][:, 0:width], w_hi[j][:, k, :], lo(k), start=False, stop=False)
                    last = pe.matmul(ps[j][:, 0:width], w_lo[j][:, k, :], hi(k), start=False, stop=(k == tiles - 1))
                last.then_inc(pe_done[j], 1)

            def stream(name, hi, lo, width, opnds, tiles=KT, step=1, fill=None, first=0, end=None):
                args = (hi, lo, width, opnds, tiles, step)
                peeled = first
                if BASE[name] == 0:
                    peeled = 1
                    for j in range(SLOTS):
                        half(name, 0, j, *args, first=True)
                elif fill:
                    peeled = 1
                    fill()
                with pe.Fori(peeled, end or ROUNDS_OF[name]) as i:
                    for j in range(SLOTS):
                        half(name, i, j, *args)

            pe.wait_ge(in_con, 32)
            stats(px[0], lambda k: sq0[:, k, :], 0)
            stats(px[1], lambda k: sq0[:, k, :], KT)
            pe.wait_ge(cc_ready, 1)
            first_modulation()
            both = (lambda k: h_hi[:, :, k, :], lambda k: h_lo[:, :, k, :])
            own = (lambda k: h_hi[:, 1, k, :], lambda k: h_lo[:, 1, k, :])
            stream("xb", *both, 2 * T, OPND["h0"], step=2)
            stream("vavg", *own, T, None)
            stream("ga", *own, T, None)

            def gates(pair):
                name, j = GATE_SLOT[pair]
                pe.wait_ge(lo_ready[j], BASE[name] + 1)
                for e in range(2):
                    head = 2 * pair + e
                    for b in range(4):
                        if head:
                            pe.wait_ge(gates_out, 4 * (head - 1) + b + 1)
                        k = 4 * e + b
                        o = px[b][:, :]
                        pe.matmul(o, w_hi[j][:, k, :], u_hi[:, head, :, :], start=True, stop=False)
                        pe.matmul(o, w_hi[j][:, k, :], u_lo[:, head, :, :], start=False, stop=False)
                        last = pe.matmul(o, w_lo[j][:, k, :], u_hi[:, head, :, :], start=False, stop=True)
                        if e == 0 or b < 3:
                            last.then_inc(gates_pe, 1)
                    if e == 1:
                        last.then_inc(pe_done[j], 1)

            def gb_tiles(name):
                for phase_name, j in GB_SLOT:
                    if phase_name == name:
                        half(name, 0, j, *own, T)

            pe.wait_ge(opnd, OPND["u"] + KT)
            gates(0)
            gb_tiles("g0")

            def taps(i, first=False, last_round=False):
                for j in range(SLOTS):
                    pe.wait_ge(lo_ready[j], i + (BASE["cv"] + 1))
                    if first:
                        pe.wait_ge(ps_free[j], BASE["cv"])
                        pe.wait_ge(opnd, OPND["cv"] + j + 1)
                    for k in range(8):
                        hi, lo = (a[:, j, bass.ds(i * 8 + k, T)] for a in (cv_hi, cv_lo))
                        pe.matmul(ps[j][:, 0:T], w_hi[j][:, k, :], hi, start=(first and k == 0), stop=False)
                        pe.matmul(ps[j][:, 0:T], w_hi[j][:, k, :], lo, start=False, stop=False)
                        last = pe.matmul(ps[j][:, 0:T], w_lo[j][:, k, :], hi, start=False,
                                         stop=(last_round and k == 7))
                    last.then_inc(pe_done[j], 1)

            taps(0, first=True)
            with pe.Fori(1, ROUNDS_OF["cv"] - 1) as i:
                taps(i)
            taps(ROUNDS_OF["cv"] - 1, last_round=True)

            pe.wait_ge(gates_out, 8)
            stats(px[0], lambda k: conv[:, k, :], 0, ln_sq)
            stats(px[1], lambda k: lnsq[:, k, :], 0, ln_sq)
            pe.wait_ge(var_ready, 3)
            gates(1)
            gb_tiles("g1")
            gb_tiles("g2")
            ya = (lambda k: ya_hi[:, k, :], lambda k: ya_lo[:, k, :])

            def gates_between():
                gates(2)
                half("ya", 0, 0, *ya, T, OPND["ya"])
                half("ya", 0, 1, *ya, T)
                gates(3)
                half("ya", 0, 2, *ya, T)
                half("ya", 0, 3, *ya, T)

            stream("ya", *ya, T, None, fill=gates_between)
            stream("yb", lambda k: yb_hi[:, k, :], lambda k: yb_lo[:, k, :], T, OPND["yb"])

            stats(px[0], lambda k: sq1[:, k, :], 2 * KT)
            h1 = (lambda k: h1_hi[:, k, :], lambda k: h1_lo[:, k, :])
            stream("od_u", *h1, T, OPND["h1"])
            stream("od_g", *h1, T, None)

            def pair_stream(name, hi, lo, ready):
                with pe.Fori(0, ROUNDS_OF[name]) as i:
                    for j in range(SLOTS):
                        pe.wait_ge(lo_ready[j], i + (BASE[name] + 1))
                        pe.wait_ge(ps_free[j], i + BASE[name])
                        ready(i, j)
                        for e in range(2):
                            o = ps[j][:, e * T:(e + 1) * T]
                            for k in range(4):
                                pe.matmul(o, w_hi[j][:, 4 * e + k, :], hi(i, j, k), start=(k == 0), stop=False)
                                pe.matmul(o, w_hi[j][:, 4 * e + k, :], lo(i, j, k), start=False, stop=False)
                                last = pe.matmul(o, w_lo[j][:, 4 * e + k, :], hi(i, j, k), start=False, stop=(k == 3))
                        last.then_inc(pe_done[j], 1)

            pair_stream("grp", lambda i, j, k: d_hi[:, i * 8 + (4 * (j // 2) + k), :],
                        lambda i, j, k: d_lo[:, i * 8 + (4 * (j // 2) + k), :],
                        lambda i, j: pe.wait_ge(opnd, i * 2 + (OPND["d"] + 1 + j // 2)))
            stats(px[1], lambda k: sqc[:, k, :], 3 * KT)
            for name, k0 in (("oda", 0), ("odb", 8)):
                pe.wait_ge(opnd, OPND["y"] + (4 if k0 == 0 else 8))
                stream(name, lambda k: y_hi[:, k0 + k, :], lambda k: y_lo[:, k0 + k, :], T, None)

            both2 = (lambda k: h2_hi[:, :, k, :], lambda k: h2_lo[:, :, k, :])
            own2 = (lambda k: h2_hi[:, 0, k, :], lambda k: h2_lo[:, 0, k, :])
            def context_first():
                for s in (1, 0):
                    for j in range(SLOTS):
                        if s:
                            pe.wait_ge(lo_ready[j], BASE["f"] + 1)
                            pe.wait_ge(ps_free[j], BASE["f"])
                        o = ps[j][:, s * T:(s + 1) * T]
                        for k in range(KT):
                            if j == 0:
                                pe.wait_ge(opnd, OPND["hc2" if s else "h2"] + k + 1)
                            pe.matmul(o, w_hi[j][:, k, :], h2_hi[:, s, k, :], start=(k == 0), stop=False)
                            pe.matmul(o, w_hi[j][:, k, :], h2_lo[:, s, k, :], start=False, stop=False)
                            last = pe.matmul(o, w_lo[j][:, k, :], h2_hi[:, s, k, :], start=False, stop=(k == KT - 1))
                        if s == 0:
                            last.then_inc(pe_done[j], 1)
                        elif j == 0:
                            stats(px[0], lambda k: sq2[:, k, :], 4 * KT)
                        elif j == SLOTS - 1:
                            stats(px[2], lambda k: sqc[:, k, :], 5 * KT)

            stream("f", *both2, 2 * T, None, fill=context_first)
            stream("i", *both2, 2 * T, None)
            for s in range(2):
                for n in range(2):
                    for h in range(HEADS):
                        if s == 0 and n == 0:
                            pe.wait_ge(ps_free[h], BASE["i"] + 1)
                        last = pe.transpose(px[2 * s + n][:, h * P:(h + 1) * P], V[:, h, s, n * P:(n + 1) * P], ident)
                    last.then_inc(hg_pe, 1)
            stream("q", *own2, T, None)
            stream("uvo", *own2, T, None)

            def direction(d):
                A, B = 4 + 4 * d, 9 * d

                def keys(s):
                    for n in range(2):
                        pe.wait_ge(hg_act, 4 + 4 * d)
                        for h in range(2):
                            for tile in range(2):
                                last = pe.transpose(px[n][:, (2 * h + tile) * P:(2 * h + tile + 1) * P],
                                                    Kk[:, d, 2 * n + h, s, tile * P:(tile + 1) * P], ident)
                        last.then_inc(hg_pe, 1)

                pe.wait_ge(hg_dve, B + 1)
                keys(1)
                pe.wait_ge(hg_act, A + 2)
                for h in range(HEADS):
                    for tile in range(2):
                        last = pe.matmul(px[0][:, h * P:(h + 1) * P], kdT[:, h, tile, :], vtok[:, 1, tile, h, :],
                                         start=(tile == 0), stop=(tile == 1))
                last.then_inc(hg_pe, 1)
                pe.wait_ge(hg_dve, B + 5)
                keys(0)
                pe.wait_ge(hg_act, A + 4)
                order = (0, 1, 2) if d == 0 else (3, 2, 1)
                for n, c in enumerate(order):
                    if n == 1:
                        pe.wait_ge(hg_dve, B + 6)
                    rows = slice((c % 2) * CHUNK, (c % 2 + 1) * CHUNK)
                    for h in range(HEADS):
                        last = pe.matmul(px[n % 2][:, h * P:(h + 1) * P], kdT[rows, h, c // 2, :],
                                         vtok[rows, 0, c // 2, h, :], start=True, stop=True)
                    last.then_inc(hg_pe, 1)
                pe.wait_ge(hg_dve, B + 8)
                for h in range(HEADS):
                    for tile in range(2):
                        t = slice(tile * P, (tile + 1) * P)
                        r = 2 * (h % 2) + tile
                        last = pe.matmul(px[h // 2][:, r * P:(r + 1) * P], ki[:, h, t], qi[:, h, t], start=True,
                                         stop=True)
                last.then_inc(hg_pe, 1)
                pe.wait_ge(hg_dve, B + 9)
                for h in range(HEADS):
                    for tile in range(2):
                        o = px[2 + h // 2][:, (h % 2) * T + tile * P:(h % 2) * T + (tile + 1) * P]
                        pe.matmul(o, vtok[:, 0, tile, h, :], sc[:, 2 * h + tile, :],
                                  start=(d == 0 and h % 2 == 0 and tile == 0), stop=False, skip_group_check=True)
                    for c in range(CHUNKS):
                        t = slice(c * CHUNK, (c + 1) * CHUNK)
                        o = px[2 + h // 2][:, (h % 2) * T + c * CHUNK:(h % 2) * T + (c + 1) * CHUNK]
                        last = pe.matmul(o, St[:, c, h, :], tq[:, h, t], start=False, stop=True,
                                         skip_group_check=True)
                last.then_inc(hg_pe, 1)

            direction(0)
            pe.wait_ge(sg_act, 1)
            for n, src in ((0, v2), (1, vsq)):
                for g in range(HEADS):
                    last = pe.matmul(px[n][:, 0:T], ones, src[:, g, :], start=(g == 0), stop=(g == HEADS - 1))
                last.then_inc(sg_pe, 1)
            stream("ga2", *own2, T, None)
            pe.wait_ge(sg_dve, 1)
            for c in range(2):
                for g in range(HEADS):
                    last = pe.transpose(px[c][:, g * P:(g + 1) * P], vn[:, g, c * P:(c + 1) * P], ident)
                last.then_inc(sg_pe, 1)
            pe.wait_ge(sg_act, 3)
            direction(1)
            pe.wait_ge(in_sgu, 48)
            for g in range(HEADS):
                for c in range(2):
                    o = px[g // 2][:, (g % 2) * T + c * P:(g % 2) * T + (c + 1) * P]
                    pe.matmul(o, vt[:, c, g, :], wsT[:, g, :], start=True, stop=False)
                    last = pe.matmul(o, ones[0:1, :], bsr[0:1, g * P:(g + 1) * P], start=False, stop=True)
            last.then_inc(sg_pe, 1)
            stream("gb2", *own2, T, None, end=1)

            pe.wait_ge(sg_dve, 2)
            for n in range(2):
                pe.wait_ge(sg_act, 4)
                pe.matmul(px[n][:, :], ones, osq[:, 2 * n:2 * n + 2, :], start=True, stop=True).then_inc(sg_pe, 1)
            stream("gb2", *own2, T, None, first=1)

            def ab(part):
                return lambda i, j, k: ((oa_hi, oa_lo), (ob_hi, ob_lo))[j % 2][part][:, k, :]

            pair_stream("pab", ab(0), ab(1), lambda i, j: pe.wait_ge(opnd, OPND["oa"] + 1))
            pe.wait_ge(opnd, OPND["m"] + 4)
            stream("wo", lambda k: m_hi[:, k, :], lambda k: m_lo[:, k, :], T, None)
            stats(px[0], lambda k: sq4[:, k, :], 6 * KT)
            stream("up", lambda k: h3_hi[:, k, :], lambda k: h3_lo[:, k, :], T, OPND["h3"])
            for name, k0, n in (("dna", 0, 8), ("dnb", 8, 8), ("dnc", 16, 6)):
                pe.wait_ge(opnd, OPND["ff"] + k0 + n)
                stream(name, lambda k: ff_hi[:, k0 + k, :], lambda k: ff_lo[:, k0 + k, :], T, None, n)
            stats(px[0], lambda k: sq5[:, k, :], 7 * KT)

        @block.scalar
        def _(act):
            S = Steps(act, act_step)

            def hi(r, j):
                act.wait_ge(raw_in[j], (r + 1) * 16)
                act.activation(w_hi[j][:], raw[j][:], ACT.Copy).then_inc(hi_ready[j], 1)

            def phase(name, evac=None, last_round=False, first=0, end=None):
                n = (end or ROUNDS_OF[name]) - (1 if last_round else 0)
                if n > first:
                    with act.Fori(first, n) as i:
                        for j in range(SLOTS):
                            act.wait_ge(pe_done[j], i + (BASE[name] + 1))
                            if evac:
                                evac(i, j)
                            hi(i + (BASE[name] + 1), j)
                if last_round:
                    for j in range(SLOTS):
                        act.wait_ge(pe_done[j], BASE[name] + n + 1)
                        if evac:
                            evac(n, j)

            act.wait_ge(in_cc, 16)
            act.activation(ccs, ccs, ACT.Silu).then_inc(cc_ready, 1)
            act.wait_ge(in_ctx, 16)
            for k in range(KT):
                act.activation(sq0[:, k, :], ctxT[:, k, :], ACT.Square).then_inc(sq_ready, 1)
            act.wait_ge(in_x, 16)
            act.wait_ge(stat_done, 1)
            for k in range(KT):
                act.activation(sq0[:, k, :], x[:, k, :], ACT.Square).then_inc(sq_ready, 1)
            act.wait_ge(softplus_in, 1)
            act.activation(lam_t[0], lam_t[0], ACT.Exp).then_inc(softplus_ex, 1)
            for n in range(2):
                act.wait_ge(var_ready, n + 1)
                act.activation(t0[:, n, :], t0[:, n, :], ACT.Sqrt).then_inc(sd_ready, 1)
            for n in range(SLOTS):
                act.wait_ge(mod0_rows, n + 1)
                act.activation(mrow[0:2, n * 2 * T:(n + 1) * 2 * T], ps[n][0:2, :], ACT.Copy).then_inc(mod0_out, 1)
            for j in range(SLOTS):
                hi(0, j)
            act.wait_ge(modc_ready, 1)
            for k in range(KT):
                for n, (src, w) in enumerate(((ctxT, 1), (sq0, 0))):
                    act.wait_ge(xn_ready, KT * n + k + 1)
                    act.activation(h_hi[:, n, k, :], src[:, k, :], ACT.Identity, scale=modA[w][:, k:k + 1],
                                   bias=modS[w][:, k:k + 1]).then_inc(h0_hi, 1)

            act.wait_ge(in_crow, 32)
            act.activation(c_row[:, 0:2, :], c_row[:, 0:2, :], ACT.Silu).then_inc(crow_ready, 1)

            def hi_tiles(count, dst, src, shift):
                for k in range(KT):
                    act.wait_ge(pre_ready, count + k + 1)
                    act.activation(dst(k), src[:, k, :], ACT.Identity, bias=shift[:, k:k + 1]).then_inc(act_hi, 1)

            def xb(i, j):
                act.activation(xpad[:, i * SLOTS + j, :, SCONV_LEFT:SCONV_LEFT + T],
                               ps[j][:].rearrange("p (s t) -> p s t", s=2), ACT.Copy).then_inc(ps_free[j], 1)

            def vavg(dst, tile0):
                def evac(i, j):
                    tile = i * 2 + j // 2
                    if j % 2 == 0:
                        act.activation(dst[:, tile - tile0, CONV_LEFT:CONV_LEFT + T], ps[j][:, 0:T], ACT.Copy) \
                           .then_inc(ps_free[j], 1)
                    else:
                        act.activation(conv[:, tile, :], ps[j][:, 0:T], ACT.Sigmoid).then_inc(ps_free[j], 1)
                return evac

            def silu_to(dst):
                def evac(i, j):
                    act.activation(dst[:, i * SLOTS + j, :], ps[j][:, 0:T], ACT.Silu).then_inc(ps_free[j], 1)
                return evac

            phase("xb", xb)
            phase("vavg", vavg(upad, 0), end=2)
            phase("vavg", vavg(va_in, CV), first=2)
            act.wait_ge(opnd, OPND["u"] + KT)
            phase("ga", silu_to(ga))

            def gb_out(name):
                for tile, (phase_name, j) in enumerate(GB_SLOT):
                    if phase_name == name:
                        act.wait_ge(pe_done[j], BASE[name] + 1)
                        act.activation(gb[:, tile, :], ps[j][:, 0:T], ACT.Silu).then_inc(ps_free[j], 1)
                        hi(BASE[name] + 1, j)

            def sigmoids(p):
                name, j = GATE_SLOT[p]
                if p in (1, 3):
                    act.wait_ge(lru_free, 2 if p == 1 else 4)
                for head in (2 * p, 2 * p + 1):
                    for g in range(4):
                        if head % 2 and g == 3:
                            act.wait_ge(pe_done[j], BASE[name] + 1)
                        else:
                            act.wait_ge(gates_pe, 7 * p + 4 * (head % 2) + g + 1)
                        d, dst, bias = g // 2, (li if g % 2 else lr), ("ev_b_i" if g % 2 else "ev_b_r")
                        act.activation(dst[:, PAIR_BUF[p] + head % 2, d, :], px[g][:, :], ACT.Sigmoid,
                                       bias=col(bias, KT * d + head)).then_inc(gates_out, 1)
                act.sem_inc(ps_free[j], 1)
                hi(BASE[name] + 1, j)

            def exps_of(p):
                act.wait_ge(gates_out, 8 * p + 8)
                act.wait_ge(lru_cols, 1)
                for head in (2 * p, 2 * p + 1):
                    for d in range(2):
                        c = slice(KT * d + head, KT * d + head + 1)
                        act.activation(la[:, d, head, :], lr[:, PAIR_BUF[p] + head % 2, d, :], ACT.Exp,
                                       scale=lru_nz[:, c]).then_inc(exp_ready, 1)
                for head in (2 * p, 2 * p + 1):
                    for d in range(2):
                        c = slice(KT * d + head, KT * d + head + 1)
                        act.wait_ge(exp_ready, 2 * head + d + 1)
                        r = lr[:, PAIR_BUF[p] + head % 2, d, :]
                        act.activation(r, r, ACT.Tanh, scale=lru_z[:, c]).then_inc(tanh_ready, 1)

            def roots(p):
                for head in (2 * p, 2 * p + 1):
                    act.wait_ge(prod_ready, head + 1)
                    r = lr[:, PAIR_BUF[p] + head % 2]
                    act.activation(r, r, ACT.Sqrt).then_inc(root_ready, 1)

            def ya_next(j):
                act.wait_ge(pe_done[j], BASE["ya"] + 1)
                hi(BASE["ya"] + 1, j)

            sigmoids(0)
            gb_out("g0")
            exps_of(0)
            phase("cv", end=ROUNDS_OF["cv"] - 1)
            roots(0)
            for j in range(SLOTS):
                act.wait_ge(pe_done[j], BASE["cv"] + ROUNDS_OF["cv"])
                act.activation(conv[:, CV + j, :], ps[j][:, 0:T], ACT.Identity, bias=col("ev_conv_b", CV + j)) \
                   .then_inc(ps_free[j], ROUNDS_OF["cv"])
                hi(BASE["g1"], j)

            for s in range(MOD_SLOTS):
                act.wait_ge(modw_used[s], 8)
            for k in range(KT):
                if k < CV:
                    act.wait_ge(conv_done, k + 1)
                else:
                    act.wait_ge(ps_free[k - CV], BASE["g1"])
                act.activation(lnsq[:, k, :], conv[:, k, :], ACT.Square).then_inc(ln_sq, 1)
            act.wait_ge(var_ready, 3)
            act.activation(lnt[:, 3, :], lnt[:, 3, :], ACT.Sqrt).then_inc(sd_ready, 1)
            sigmoids(1)
            exps_of(1)
            gb_out("g1")
            for k in range(KT):
                act.wait_ge(ln_norm, k + 1)
                act.activation(conv[:, k, :], conv[:, k, :], ACT.Silu, scale=col("ev_ln_g", k),
                               bias=col("ev_ln_b", k)).then_inc(ln_silu, 1)
            gb_out("g2")
            sigmoids(2)
            roots(1)
            exps_of(2)
            sigmoids(3)
            roots(2)
            exps_of(3)
            ya_next(0)
            ya_next(1)
            roots(3)
            ya_next(2)
            ya_next(3)

            def squares(name, dst):
                def evac(i, j):
                    act.wait_ge(ps_free[j], i + (BASE[name] + 1))
                    act.activation(dst[:, i * SLOTS + j, :], x[:, i * SLOTS + j, :], ACT.Square).then_inc(sq_ready, 1)
                return evac

            def phase_sq(name, dst, last_round=False):
                n = ROUNDS_OF[name] - (1 if last_round else 0)
                with act.Fori(0, n) as i:
                    for j in range(SLOTS):
                        act.wait_ge(pe_done[j], i + (BASE[name] + 1))
                        hi(i + (BASE[name] + 1), j)
                    for j in range(SLOTS):
                        squares(name, dst)(i, j)
                if last_round:
                    for j in range(SLOTS):
                        squares(name, dst)(n, j)

            phase("ya", first=1)
            phase_sq("yb", sq1)

            def sqrt_of(n, t):
                act.activation(warm, warm, ACT.Sqrt).then_inc(act_step, 1)
                S.n += 1
                act.wait_ge(var_ready, n)
                S.sync()
                act.activation(t, t, ACT.Sqrt).then_inc(sd_ready, 1)

            sqrt_of(4, vr1[:])
            hi_tiles(0, lambda k: h1_hi[:, k, :], t1, shift1)
            act.wait_ge(in_crow2, 16)
            act.activation(c_row[:, 2, :], c_row[:, 2, :], ACT.Silu).then_inc(crow_ready, 1)

            def od_u(i, j):
                act.activation(opad[:, i * SLOTS + j, :, 8:8 + GRID_W],
                               ps[j][:, 0:T].rearrange("p (r c) -> p r c", c=GRID_W), ACT.Copy) \
                   .then_inc(ps_free[j], 1)

            act.wait_ge(pads_ready, 1)
            phase("od_u", od_u)
            phase("od_g", silu_to(og))
            phase("grp")
            act.wait_ge(in_ctx2, 16)
            for k in range(KT):
                act.activation(sqc[:, k, :], ctx2T[:, k, :], ACT.Square).then_inc(sq_ready, 1)
            sqrt_of(5, vr[:, 0, :])
            phase("oda")
            hi_tiles(KT, lambda k: h2_hi[:, 1, k, :], t2, sh2[1])
            phase_sq("odb", sq2)
            sqrt_of(6, vr[:, 1, :])
            for k in range(KT):
                act.wait_ge(x3_ready, k + 1)
                act.activation(sqc[:, k, :], x[:, k, :], ACT.Square).then_inc(sq_ready, 1)
            sqrt_of(7, vr[:, 2, :])
            hi_tiles(2 * KT, lambda k: h2_hi[:, 0, k, :], t2, sh2[0])
            act.wait_ge(lb_in, 1)
            act.activation(lb_t[0], lb_t[0], ACT.Exp).then_inc(lb_ex, 1)
            act.activation(lb_t[1], lb_t[1], ACT.Exp).then_inc(lb_ex, 1)

            def f_evac(i, j):
                act.activation(Lg[:, i, j, :, :], ps[j][:].rearrange("p (s t) -> p s t", s=2), ACT.Sigmoid) \
                   .then_inc(ps_free[j], 1)

            def i_evac(i, j):
                act.activation(V[:, j, :, :], ps[j][:].rearrange("p (s t) -> p s t", s=2), ACT.Copy) \
                   .then_inc(ps_free[j], 1)

            phase("f", f_evac)
            phase("i", i_evac)
            for n in range(4):
                act.wait_ge(hg_pe, n + 1)
                act.activation(vtok[:, n // 2, n % 2, :, :], px[n][:].rearrange("p (h e) -> p h e", h=HEADS),
                               ACT.Copy).then_inc(hg_act, 1)
            for d in range(2):
                act.wait_ge(fk, d + 1)
                act.activation(Lg[:, d], Lg[:, d], ACT.Ln).then_inc(logf, 1)

            def exps(d):
                act.wait_ge(hx_dve, 2 * d + 1)
                for h in range(HEADS):
                    act.activation(Lg[:, d, h, 1, :], Lg[:, d, h, 1, :], ACT.Exp, scale=-1.0,
                                   bias=tots[:, HEADS * d + h:HEADS * d + h + 1]).then_inc(hx_act, 1)
                act.activation(ki[:], tq[:], ACT.Exp, scale=-1.0).then_inc(hx_act, 1)
                act.activation(qi[:], tq[:], ACT.Exp).then_inc(hx_act, 1)
                act.activation(dec, bls, ACT.Exp).then_inc(hx_act, 1)
                act.wait_ge(hx_act, 9 * d + 6)
                act.activation(tq[:], Lg[:, d, :, 0, :], ACT.Exp).then_inc(hx_act, 1)
                act.wait_ge(hx_dve, 2 * d + 2)
                act.activation(Lg[:, d, :, 0, :], Lg[:, d, :, 0, :], ACT.Exp).then_inc(hx_act, 1)

            def keys_out(d):
                for s in range(2):
                    if s:
                        act.wait_ge(hg_pe, 4 + 10 * d + 3)
                    for n in range(2):
                        act.wait_ge(hg_pe, 4 + 10 * d + 3 * s + n + 1)
                        act.activation(kdT[:, 2 * n:2 * n + 2, :, :],
                                       px[n][:].rearrange("p (h t d) -> p h t d", h=2, t=2), ACT.Copy) \
                           .then_inc(hg_act, 1)

            def q_evac(i, j):
                act.activation(q[:, j, :], ps[j][:, 0:T], ACT.Copy).then_inc(ps_free[j], 1)

            phase("q", q_evac)
            for n, (dst, func) in enumerate(((u2, ACT.Gelu_apprx_tanh), (v2, ACT.Gelu_apprx_tanh), (og2, ACT.Silu))):
                for j in range(SLOTS):
                    act.wait_ge(pe_done[j], BASE["uvo"] + n + 1)
                    act.activation(dst[:, j, :], ps[j][:, 0:T], func).then_inc(ps_free[j], 1)
                    hi(BASE["uvo"] + n + 1, j)
                if n == 1:
                    exps(0)

            def sigmoid_to(dst):
                def evac(i, j):
                    act.activation(dst[:, i * SLOTS + j, :], ps[j][:, 0:T], ACT.Sigmoid).then_inc(ps_free[j], 1)
                return evac

            keys_out(0)
            act.activation(vsq[:], v2[:], ACT.Square).then_inc(sg_act, 1)
            sqrt_of(8, lnv[:, 3, :])
            phase("ga2", sigmoid_to(ga2), end=1)
            act.wait_ge(hg_pe, 14)
            exps(1)
            phase("ga2", sigmoid_to(ga2), first=1)
            for c in range(2):
                act.wait_ge(sg_pe, 3 + c)
                act.activation(vt[:, c, :, :], px[c][:].rearrange("p (g e) -> p g e", g=HEADS), ACT.Copy) \
                   .then_inc(sg_act, 1)
            keys_out(1)
            phase("gb2", sigmoid_to(gb2), end=1)
            act.wait_ge(hg_pe, 24)
            for n in range(2):
                a = act.activation(osq[:, 2 * n:2 * n + 2, :], px[2 + n][:].rearrange("p (h t) -> p h t", h=2),
                                   ACT.Square)
                if n:
                    a.then_inc(sg_act, 1)
                else:
                    S.do(a)
            sqrt_of(9, ors[:])
            phase("gb2", sigmoid_to(gb2), first=1)
            phase("pab")
            phase_sq("wo", sq4)
            sqrt_of(10, v4[:, 0, :])
            hi_tiles(3 * KT, lambda k: h3_hi[:, k, :], t4, sh3)

            def up(i, j):
                if j % 2 == 0:
                    act.wait_ge(ps_free[j + 1], i + BASE["up"])
                    act.activation(sa[:, j // 2, :], ps[j][:, 0:T], ACT.Silu).then_inc(ps_free[j], 1)

            phase("up", up)
            phase("dna")
            phase("dnb")
            phase_sq("dnc", sq5, last_round=True)
            sqrt_of(11, v4[:, 0, :])

        @block.vector
        def _(v):
            S = Steps(v, dve_step)

            def tt_(o, a, b, op):
                return v.tensor_tensor(o, a, b, op)

            def modulate(count, src, rstd, scale, shift, tmp, hi, lo):
                for s in range(KT + 2):
                    if s < KT:
                        v.scalar_tensor_tensor(out=tmp[:, s, :], in0=src(s), scalar=scale[:, s:s + 1], in1=rstd,
                                               op0=ALU.mult, op1=ALU.mult).then_inc(pre_ready, 1)
                    if s >= 2:
                        k = s - 2
                        v.wait_ge(act_hi, count + k + 1)
                        v.scalar_tensor_tensor(out=lo(k), in0=tmp[:, k, :], scalar=shift[:, k:k + 1],
                                               in1=hi(k).bitcast(F32), op0=ALU.add,
                                               op1=ALU.subtract).then_inc(opnd, 1)

            def mod_tiles(g, row):
                for s in range(MOD_SLOTS):
                    q = g * MOD_SLOTS + s
                    v.wait_ge(modw_in[s], 16 * (g + 1))
                    v.scalar_tensor_tensor(out=modw[s][:], in0=modw[s][:], scalar=1.0, in1=c_row[:, row, :],
                                           op0=ALU.mult, op1=ALU.mult,
                                           accum_out=mod[:, q:q + 1]).then_inc(modw_used[s], 1)

            v.wait_ge(in_con, 32)
            S.do(v.memset(warm, 1.0))

            lam = col("ev_lam", 0, 2 * KT)
            S.do(v.tensor_scalar(lam_t[1], lam, -1.0, None, ALU.mult))
            S.sync()
            v.tensor_tensor(lam_t[0], lam, lam_t[1], ALU.min).then_inc(softplus_in, 1)
            v.wait_ge(softplus_ex, 1)
            S.do(v.tensor_scalar(lam_t[2], lam_t[0], 2.0, None, ALU.add))
            S.sync()
            S.do(v.reciprocal(lam_t[2], lam_t[2]))
            S.sync()
            S.do(tt_(lam_t[0], lam_t[0], lam_t[2], ALU.mult))
            S.sync()
            S.do(tt_(lam_t[2], lam_t[0], lam_t[0], ALU.mult))
            S.sync()
            S.do(v.tensor_scalar(lam_t[3], lam_t[2], 1 / 17, 1 / 15, ALU.mult, ALU.add))
            for m in (13, 11, 9, 7, 5, 3, 1):
                S.sync()
                S.do(tt_(lam_t[3], lam_t[3], lam_t[2], ALU.mult))
                S.sync()
                S.do(v.tensor_scalar(lam_t[3], lam_t[3], 1 / m, None, ALU.add))
            S.sync()
            S.do(tt_(lam_t[3], lam_t[3], lam_t[0], ALU.mult))
            S.do(v.tensor_scalar(lam_t[1], lam_t[1], 0.0, 8.0, ALU.max, ALU.mult))
            S.sync()
            S.do(v.scalar_tensor_tensor(out=lru_z, in0=lam_t[3], scalar=16.0, in1=lam_t[1], op0=ALU.mult,
                                        op1=ALU.add))
            S.sync()
            v.tensor_scalar(lru_nz, lru_z, -1.0, None, ALU.mult).then_inc(lru_cols, 1)

            for n in range(2):
                v.wait_ge(stat_done, n + 1)
                v.tensor_scalar(t0[:, n, :], px[n][:, 0:T], 1.0 / D, EPS6, ALU.mult, ALU.add).then_inc(var_ready, 1)
            rs = [conv[:, n, :] for n in range(2)]
            for n in range(2):
                v.wait_ge(sd_ready, n + 1)
                S.do(v.reciprocal(rs[n], t0[:, n, :]))
            S.sync()
            for n, src in enumerate((ctxT, x)):
                dst = (ctxT, sq0)[n]
                for k in range(KT):
                    v.tensor_tensor(dst[:, k, :], src[:, k, :], rs[n], ALU.mult).then_inc(xn_ready, 1)

            v.wait_ge(mod0_done, 1)
            for w in range(2):
                S.do(tt_(mod0[:, :, w], px[3][:, w:4 * KT:2], col("mod_b", 0, 2 * KT), ALU.add))
            S.sync()
            for w in range(2):
                S.do(v.tensor_scalar(modS[w], mod0[:, 0:KT, w], 1.0, None, ALU.mult))
                a = v.scalar_tensor_tensor(out=modA[w], in0=mod0[:, KT:2 * KT, w], scalar=1.0,
                                           in1=col("norm_g", 0, KT), op0=ALU.add, op1=ALU.mult)
                if w:
                    a.then_inc(modc_ready, 1)
                else:
                    S.do(a)
            v.wait_ge(modc_ready, 1)
            v.wait_ge(xn_ready, 2 * KT)

            for s in range(2 * KT + 1):
                if s < 2 * KT:
                    k, n = s // 2, s % 2
                    if s >= 4:
                        v.wait_ge(opnd, OPND["h0"] + s - 3)
                    S.do(v.tensor_scalar(t0[:, s % 4, :], (ctxT, sq0)[n][:, k, :], modA[1 - n][:, k:k + 1],
                                         modS[1 - n][:, k:k + 1], ALU.mult, ALU.add))
                if s:
                    k, n = (s - 1) // 2, (s - 1) % 2
                    S.sync(S.n - (1 if s < 2 * KT else 0))
                    v.wait_ge(h0_hi, s)
                    v.tensor_tensor(h_lo[:, n, k, :], t0[:, (s - 1) % 4, :], h_hi[:, n, k, :].bitcast(F32),
                                    ALU.subtract).then_inc(opnd, 1)
            v.wait_ge(opnd, OPND["h0"] + 2 * KT)
            S.do(v.memset(xpad[:, :, :, 0:SCONV_LEFT], 0.0))
            S.do(v.memset(xpad[:, :, :, SCONV_LEFT + T:XW], 0.0))
            S.do(v.memset(upad[:, :, 0:CONV_LEFT], 0.0))
            S.do(v.memset(upad[:, :, CONV_LEFT + T:UW], 0.0))
            S.do(v.memset(cv_hi[:, :, 0:CONV_LEFT].bitcast(F32), 0.0))
            S.do(v.memset(cv_hi[:, :, CONV_LEFT + T:UW].bitcast(F32), 0.0))

            S.sync()
            v.wait_ge(crow_ready, 1)
            for i in S.loop(ROUNDS_OF["xb"], 5 * SLOTS):
                for j in range(SLOTS):
                    tile = i * SLOTS + j
                    v.wait_ge(ps_free[j], i + 1)
                    tmp = stmp[:, j]

                    def tap(n):
                        c0 = COL["ev_sconv_w"] + KT * n
                        return xpad[:, tile, :, n:n + T], cols[:, bass.ds(tile + c0, 1)]

                    src, w = tap(0)
                    S.do(v.tensor_scalar(tmp, src, w, cols[:, bass.ds(tile + COL["ev_sconv_b"], 1)], ALU.mult,
                                         ALU.add))
                    for n in (1, 3):
                        src, w = tap(n)
                        S.sync()
                        S.do(v.scalar_tensor_tensor(out=tmp, in0=src, scalar=w, in1=tmp, op0=ALU.mult, op1=ALU.add))
                    src, w = tap(SCONV_LEFT)
                    S.sync()
                    S.do(v.scalar_tensor_tensor(out=src, in0=src, scalar=w, in1=tmp, op0=ALU.mult, op1=ALU.add))
                    S.sync()
                    S.do(v.tensor_copy(u_hi[:, tile], src))
                    S.sync()
                    v.tensor_tensor(u_lo[:, tile], src, u_hi[:, tile].bitcast(F32), ALU.subtract).then_inc(opnd, 1)
                    v.wait_ge(modw_in[j], i * 16 + 16)
                    v.scalar_tensor_tensor(out=modw[j][:], in0=modw[j][:], scalar=1.0, in1=c_row[:, 0, :],
                                           op0=ALU.mult, op1=ALU.mult,
                                           accum_out=mod[:, bass.ds(tile, 1)]).then_inc(modw_used[j], 1)

            def convolve(pair):
                pair_tiles = (2 * pair, 2 * pair + 1)
                for e, tile in enumerate(pair_tiles):
                    v.wait_ge(ps_free[2 * e], BASE["vavg"] + pair + 1)
                    v.wait_ge(ps_free[2 * e + 1], BASE["vavg"] + pair + 1)
                    mid = upad[:, tile, CONV_LEFT:CONV_LEFT + T]
                    S.do(tt_(mid, mid, conv[:, tile, :], ALU.mult))
                for n in range(CONV_TAPS):
                    for e, tile in enumerate(pair_tiles):
                        src = upad[:, tile, n:n + T]
                        w = col("ev_conv_w", KT * n + tile)
                        S.sync(S.n if n == CONV_TAPS - 1 and e else S.n - 1)
                        if n == 0:
                            S.do(v.tensor_scalar(conv[:, tile, :], src, w, col("ev_conv_b", tile), ALU.mult, ALU.add))
                            continue
                        a = v.scalar_tensor_tensor(out=conv[:, tile, :], in0=src, scalar=w, in1=conv[:, tile, :],
                                                   op0=ALU.mult, op1=ALU.add)
                        if n == CONV_TAPS - 1:
                            a.then_inc(conv_done, 1)
                        else:
                            S.do(a)

            def mods_used(g):
                for s in range(MOD_SLOTS):
                    v.wait_ge(modw_used[s], g)

            def affine_cols(scale, shift, g, b_name, b0, q0, src=mod):
                S.do(tt_(shift, src[:, q0:q0 + KT], col(b_name, b0, KT), ALU.add))
                S.do(tt_(scale, src[:, q0 + KT:q0 + 2 * KT], col(b_name, b0 + KT, KT), ALU.add))
                S.sync()
                S.do(v.scalar_tensor_tensor(out=scale, in0=scale, scalar=1.0, in1=g, op0=ALU.add, op1=ALU.mult))

            def lru_root(p):
                for head in (2 * p, 2 * p + 1):
                    b = PAIR_BUF[p] + head % 2
                    uf = xpad[:, head, :, SCONV_LEFT:SCONV_LEFT + T]
                    v.wait_ge(exp_ready, 2 * head + 2)
                    if head:
                        v.wait_ge(prod_ready, head)
                    S.do(tt_(asq[:], la[:, :, head, :], la[:, :, head, :], ALU.mult))
                    for d in range(2):
                        i_d = li[:, b, d, :].rearrange("p (s t) -> p s t", s=2)
                        S.do(tt_(i_d, i_d, uf, ALU.mult))
                    S.sync()
                    v.wait_ge(tanh_ready, 2 * head + 2)
                    v.scalar_tensor_tensor(out=lr[:, b], in0=asq[:], scalar=1.0, in1=lr[:, b], op0=ALU.add,
                                           op1=ALU.mult).then_inc(prod_ready, 1)

            def lru_scan(p):
                for head in (2 * p, 2 * p + 1):
                    b = PAIR_BUF[p] + head % 2
                    v.wait_ge(root_ready, head + 1)
                    S.do(tt_(li[:, b], li[:, b], lr[:, b], ALU.mult))
                S.sync()
                for head in (2 * p, 2 * p + 1):
                    h, a = li[:, PAIR_BUF[p] + head % 2], la[:, :, head, :]
                    S.do(v.tensor_tensor_scan(h[:, 1, T - 1::-1], a[:, 1, T - 1::-1], h[:, 1, T - 1::-1], 0.0,
                                              ALU.mult, ALU.add))
                    S.do(v.tensor_tensor_scan(h[:, 0, :], a[:, 0, :], h[:, 0, :], 0.0, ALU.mult, ALU.add))
                    S.sync(S.n - 1)
                    S.do(v.tensor_tensor_scan(h[:, 1, 2 * T - 1:T - 1:-1], a[:, 1, 2 * T - 1:T - 1:-1],
                                              h[:, 1, 2 * T - 1:T - 1:-1], h[:, 1, 0:1], ALU.mult, ALU.add))
                S.sync()
                for head in (2 * p, 2 * p + 1):
                    h = li[:, PAIR_BUF[p] + head % 2]
                    v.tensor_tensor(xpad[:, head, 1, SCONV_LEFT:SCONV_LEFT + T], h[:, 0, T:], h[:, 1, T:], ALU.add) \
                     .then_inc(lru_free, 1)

            def lru_out(p):
                for head in (2 * p, 2 * p + 1):
                    name, j = GB_SLOT[head]
                    v.wait_ge(ps_free[j], BASE[name] + 1)
                    v.wait_ge(lru_free, head + 1)
                    S.do(tt_(gb[:, head, :], gb[:, head, :], xpad[:, head, 1, SCONV_LEFT:SCONV_LEFT + T], ALU.mult))
                S.sync()
                for head in (2 * p, 2 * p + 1):
                    S.do(v.tensor_copy(yb_hi[:, head, :], gb[:, head, :]))
                S.sync()
                for head in (2 * p, 2 * p + 1):
                    v.tensor_tensor(yb_lo[:, head, :], gb[:, head, :], yb_hi[:, head, :].bitcast(F32), ALU.subtract) \
                     .then_inc(opnd, 1)

            convolve(0)
            mod_tiles(2, 0)
            for j in range(CV):
                for e in range(2):
                    v.wait_ge(ps_free[2 * (j % 2) + e], BASE["vavg"] + CV // 2 + j // 2 + 1)
                t = conv[:, CV + j, :]
                mid = slice(CONV_LEFT, CONV_LEFT + T)
                S.do(tt_(t, va_in[:, j, mid], t, ALU.mult))
                S.sync()
                S.do(v.memset(cv_lo[:, j, 0:CONV_LEFT].bitcast(F32), 0.0))
                S.do(v.memset(cv_lo[:, j, CONV_LEFT + T:UW].bitcast(F32), 0.0))
                S.do(v.tensor_copy(cv_hi[:, j, mid], t))
                S.sync()
                v.tensor_tensor(cv_lo[:, j, mid], t, cv_hi[:, j, mid].bitcast(F32), ALU.subtract).then_inc(opnd, 1)
            mod_tiles(3, 0)
            mod_tiles(4, 0)
            convolve(1)
            mod_tiles(5, 0)
            lru_root(0)
            mod_tiles(6, 0)
            mod_tiles(7, 0)
            lru_scan(0)
            mods_used(8)
            S.do(tt_(gate0, mod[:, 0:KT], col("mod_b", 2 * KT, KT), ALU.add))
            affine_cols(sc1, shift1, col("norm_g", KT, KT), "mod_b", 3 * KT, KT)
            S.do(tt_(gate1, mod[:, 3 * KT:4 * KT], col("mod_b", 5 * KT, KT), ALU.add))
            S.sync()

            v.wait_ge(stat_done, 3)
            S.do(v.tensor_scalar(lnt[:, 0, :], px[0][:, 0:T], 1.0 / D, None, ALU.mult))
            S.sync()
            S.do(tt_(lnt[:, 1, :], lnt[:, 0, :], lnt[:, 0, :], ALU.mult))
            v.wait_ge(stat_done, 4)
            S.do(v.tensor_scalar(lnt[:, 2, :], px[1][:, 0:T], 1.0 / D, EPS5, ALU.mult, ALU.add))
            S.sync()
            v.tensor_tensor(lnt[:, 3, :], lnt[:, 2, :], lnt[:, 1, :], ALU.subtract).then_inc(var_ready, 1)
            v.wait_ge(sd_ready, 3)
            S.do(v.reciprocal(lnt[:, 4, :], lnt[:, 3, :]))
            S.sync()
            for s in range(KT + 1):
                if s < KT:
                    S.do(tt_(conv[:, s, :], conv[:, s, :], lnt[:, 0, :], ALU.subtract))
                if s >= 1:
                    k = s - 1
                    S.sync(S.n - (1 if s < KT else 0))
                    v.tensor_tensor(conv[:, k, :], conv[:, k, :], lnt[:, 4, :], ALU.mult).then_inc(ln_norm, 1)
            lru_root(1)
            for k in range(KT):
                v.wait_ge(ln_silu, k + 1)
                v.wait_ge(ps_free[k % SLOTS], BASE["ga"] + k // SLOTS + 1)
                S.do(tt_(conv[:, k, :], conv[:, k, :], ga[:, k, :], ALU.mult))
                S.sync()
                S.do(v.tensor_copy(ya_hi[:, k, :], conv[:, k, :]))
                S.sync()
                v.tensor_tensor(ya_lo[:, k, :], conv[:, k, :], ya_hi[:, k, :].bitcast(F32), ALU.subtract) \
                 .then_inc(opnd, 1)

            def add_half(name, gate, i, j):
                v.wait_ge(pe_done[j], i + (BASE[name] + 1))
                v.wait_ge(ps_free[j], i + BASE[name])
                xt = x[:, i * SLOTS + j, :]
                v.scalar_tensor_tensor(out=xt, in0=ps[j][:, 0:T], scalar=gate[:, bass.ds(i * SLOTS + j, 1)],
                                       in1=xt, op0=ALU.mult, op1=ALU.add).then_inc(ps_free[j], 1)

            def add_to_x(name, gate, first=0):
                with v.Fori(first, ROUNDS_OF[name]) as i:
                    for j in range(SLOTS):
                        add_half(name, gate, i, j)

            lru_scan(1)
            lru_out(0)
            lru_out(1)
            for p in (2, 3):
                lru_root(p)
                lru_scan(p)
                lru_out(p)
                if p == 2:
                    add_half("ya", gate0, 0, 0)
                    add_half("ya", gate0, 0, 1)
            add_half("ya", gate0, 0, 2)
            add_half("ya", gate0, 0, 3)
            add_to_x("ya", gate0, 1)
            for j in range(SLOTS):
                v.wait_ge(ps_free[j], BASE["ya"] + 2)
            add_to_x("yb", gate0)

            def rstd(stat, bank, width, eps, t, dst, var_n):
                v.wait_ge(stat_done, stat)
                v.tensor_scalar(t, bank, 1.0 / width, eps, ALU.mult, ALU.add).then_inc(var_ready, 1)
                v.wait_ge(sd_ready, var_n)
                S.do(v.reciprocal(dst, t))
                S.sync()

            for j in range(SLOTS):
                v.wait_ge(ps_free[j], BASE["od_u"])
            S.do(v.memset(opad[:, :, :, 0:8], 0.0))
            v.memset(opad[:, :, :, 8 + GRID_W:PW], 0.0).then_inc(pads_ready, 1)
            rstd(5, px[0][:, 0:T], D, EPS6, vr1[:], vr1[:], 4)
            modulate(0, lambda k: x[:, k, :], vr1[:], sc1, shift1, t1,
                     lambda k: h1_hi[:, k, :], lambda k: h1_lo[:, k, :])
            v.wait_ge(opnd, OPND["h1"] + KT)

            def window(g):
                src = opad[:, 4 * g:4 * g + 4, :, :].rearrange("p a r c -> p (a r) c")
                w = WINDOWS[g]
                steps = [2]
                while steps[-1] < w:
                    steps.append(2 * steps[-1])
                for n, size in enumerate(steps):
                    rest = sum(m // 4 for m in steps[n + 1:])
                    lo, hi_ = 8 - rest, 8 + GRID_W + rest
                    back, ahead = (1, 0) if size == 2 else (size // 4, size // 4)
                    S.do(tt_(win[n % 2][:, :, lo:hi_], src[:, :, lo - back:hi_ - back], src[:, :, lo + ahead:hi_ + ahead],
                             ALU.add))
                    S.sync()
                    src = win[n % 2]
                return src[:, :, 8:8 + GRID_W]

            def inner(g):
                return opad[:, 4 * g:4 * g + 4, :, 8:8 + GRID_W].rearrange("p a r c -> p (a r) c")

            pdv = pd[:].rearrange("p a (r c) -> p (a r) c", c=GRID_W)
            for g in range(len(WINDOWS)):
                for j in range(SLOTS):
                    v.wait_ge(ps_free[j], BASE["od_u"] + g + 1)
                if g:
                    v.wait_ge(opnd, OPND["d"] + g)
                mean = window(g)
                c0 = CON["inv_count"] + g * GRID_W
                inv = con[:, c0:c0 + GRID_W].rearrange("p (a c) -> p a c", a=1).to_broadcast([P, 16, GRID_W])
                S.do(tt_(pdv, mean, inv, ALU.mult))
                S.sync()
                S.do(tt_(pdv, pdv, inner(g), ALU.subtract))
                S.sync()
                S.do(v.tensor_copy(d_hi[:, 4 * g:4 * g + 4, :], pd[:]))
                S.sync()
                v.tensor_tensor(d_lo[:, 4 * g:4 * g + 4, :], pd[:], d_hi[:, 4 * g:4 * g + 4, :].bitcast(F32),
                                ALU.subtract).then_inc(opnd, 1)
                if g == 0:
                    v.wait_ge(crow_ready, 2)
                for s in range(MOD_SLOTS):
                    t = (8 + g) * MOD_SLOTS + s
                    v.wait_ge(modw_in[s], 16 * (9 + g))
                    S.sync()
                    a = v.scalar_tensor_tensor(out=c_row[:, 0, :], in0=modw[s][:], scalar=1.0, in1=c_row[:, 2, :],
                                               op0=ALU.mult, op1=ALU.mult, accum_out=mod_c[:, t - 4 * KT:t - 4 * KT + 1])
                    S.do(a)
                    v.scalar_tensor_tensor(out=modw[s][:], in0=modw[s][:], scalar=1.0, in1=c_row[:, 1, :],
                                           op0=ALU.mult, op1=ALU.mult,
                                           accum_out=mod[:, t:t + 1]).then_inc(modw_used[s], 1)

            for i in S.loop(ROUNDS_OF["grp"], 2 * SLOTS):
                for j in range(SLOTS):
                    v.wait_ge(pe_done[j], i + (BASE["grp"] + 1))
                    v.wait_ge(ps_free[j], i + BASE["grp"])
                    t = i * 8 + 2 * j
                    yt = ytmp[:, j % 2]
                    for e in range(2):
                        a = v.scalar_tensor_tensor(
                            out=yt[:, e, :], in0=ps[j][:, e * T:(e + 1) * T],
                            scalar=cols[:, bass.ds(t + (COL["od_scale"] + e), 1)],
                            in1=og[:, t + e, :], op0=ALU.mult, op1=ALU.mult)
                        if e:
                            a.then_inc(ps_free[j], 1)
                        else:
                            S.do(a)
                    S.sync()
                    v.wait_ge(ps_free[j], i + (BASE["grp"] + 1))
                    S.do(v.tensor_copy(y_hi[:, bass.ds(t, 2), :], yt))
                    S.sync()
                    v.tensor_tensor(y_lo[:, bass.ds(t, 2), :], yt, y_hi[:, bass.ds(t, 2), :].bitcast(F32), ALU.subtract) \
                     .then_inc(opnd, 1)
            mods_used(12)
            affine_cols(sc2[0], sh2[0], col("g_mix_2", 0, KT), "b_mod_2", 0, 4 * KT)
            affine_cols(sc2[1], sh2[1], col("g_mix_2", 0, KT), "b_mod_2", 0, 0, mod_c)
            rstd(6, px[1][:, 0:T], D, EPS, vr[:, 0, :], vr[:, 3, :], 5)
            add_to_x("oda", gate1)
            v.wait_ge(ps_free[3], BASE["oda"] + 2)
            modulate(KT, lambda k: ctx2T[:, k, :], vr[:, 3, :], sc2[1], sh2[1], t2, lambda k: h2_hi[:, 1, k, :], lambda k: h2_lo[:, 1, k, :])
            add_to_x("odb", gate1)

            rstd(7, px[0][:, 0:T], D, EPS6, vr[:, 1, :], vr[:, 0, :], 6)
            for k in range(KT):
                v.scalar_tensor_tensor(out=x[:, k, :], in0=x[:, k, :], scalar=col("final_g", k), in1=vr[:, 0, :],
                                       op0=ALU.mult, op1=ALU.mult).then_inc(x3_ready, 1)
            v.wait_ge(x3_ready, KT)
            rstd(8, px[2][:, 0:T], D, EPS, vr[:, 2, :], vr[:, 1, :], 7)
            modulate(2 * KT, lambda k: x[:, k, :], vr[:, 1, :], sc2[0], sh2[0], t2, lambda k: h2_hi[:, 0, k, :], lambda k: h2_lo[:, 0, k, :])
            n = 2 * HEADS
            g0, g1 = col("lb_gamma_2", 0, n), col("lb_gamma_2", n, n)
            S.do(tt_(lb_t[2], g0, g1, ALU.max))
            S.sync()
            S.do(tt_(lb_t[0], g0, lb_t[2], ALU.subtract))
            v.tensor_tensor(lb_t[1], g1, lb_t[2], ALU.subtract).then_inc(lb_in, 1)
            v.wait_ge(lb_ex, 2)
            S.do(tt_(lb_t[1], lb_t[0], lb_t[1], ALU.add))
            S.sync()
            S.do(v.reciprocal(lb_t[1], lb_t[1]))
            S.sync()
            S.do(tt_(lb, lb_t[0], lb_t[1], ALU.mult))
            S.sync()
            S.do(v.tensor_scalar(oml, lb, -1.0, 1.0, ALU.mult, ALU.add))
            S.sync()
            S.do(v.tensor_scalar(noml, oml, -1.0, None, ALU.mult))
            S.sync()
            for g in range(12, 16):
                mod_tiles(g, 1)
            for d in range(2):
                for h in range(HEADS):
                    v.wait_ge(ps_free[h], BASE["f"] + d + 1)
                    c = slice(HEADS * d + h, HEADS * d + h + 1)
                    S.do(v.tensor_scalar(Kk[:, d, h], Lg[:, d, h], noml[:, c], oml[:, c], ALU.mult, ALU.add))
                S.sync()
                for h in range(HEADS):
                    c = slice(HEADS * d + h, HEADS * d + h + 1)
                    a = v.tensor_scalar(Lg[:, d, h], Lg[:, d, h], oml[:, c], lb[:, c], ALU.mult, ALU.add)
                    if h == HEADS - 1:
                        a.then_inc(fk, 1)
                    else:
                        S.do(a)


            mod_tiles(16, 1)

            def scans(d):
                v.wait_ge(logf, d + 1)
                along = slice(None) if d == 0 else slice(None, None, -1)
                starts = con[:, CON["restart_b" if d else "restart_f"]:][:, 0:T]
                all_on = con[:, CON["ones"]:CON["ones"] + T]
                for h in range(HEADS):
                    for s, keep in ((0, starts), (1, all_on)):
                        S.do(v.tensor_tensor_scan(Lg[:, d, h, s, along], keep[:, along], Lg[:, d, h, s, along], 0.0,
                                                  ALU.mult, ALU.add))
                S.sync()

            def chunks(a):
                return a.rearrange("p h (c t) -> p h c t", t=CHUNK)

            def wide(c):
                return c.rearrange("p (h n a) -> p h n a", h=HEADS, a=1).to_broadcast([P, HEADS, CHUNKS, CHUNK])

            def direction(d):
                at_end = CHUNK - 1 if d == 0 else 0
                e0, g0_ = 9 * d, 4 + 10 * d
                Lx, Lc = chunks(Lg[:, d, :, 0, :]), Lg[:, d, :, 1, :]
                if d:
                    v.wait_ge(hg_pe, 14)
                S.do(v.tensor_copy(tots[:, HEADS * d:HEADS * d + HEADS], Lc[:, :, T - 1 if d == 0 else 0]))
                S.do(v.tensor_copy(bls.rearrange("p (h c) -> p h c", h=HEADS), Lx[:, :, :, at_end]))
                S.do(v.memset(sc[:], 0.0))
                S.sync()
                S.do(v.tensor_scalar(mids, bls, 0.5, None, ALU.mult))
                S.sync()
                v.tensor_tensor(chunks(tq[:]), Lx, wide(mids), ALU.subtract).then_inc(hx_dve, 1)
                if d:
                    normalise_v()
                else:
                    mod_tiles(17, 1)
                v.wait_ge(hx_act, e0 + 8)
                v.tensor_tensor(Lx, wide(bls), Lx, ALU.subtract).then_inc(hx_dve, 1)
                Kc, Kx = Kk[:, d, :, 1, :], Kk[:, d, :, 0, :]
                v.tensor_tensor(Kc, Kc, Lc, ALU.mult).then_inc(hg_dve, 1)
                S.do(tt_(ki[:], ki[:], Kx, ALU.mult))
                for j in range(SLOTS):
                    v.wait_ge(ps_free[j], BASE["q"] + 1)
                v.tensor_tensor(qi[:], qi[:], q[:], ALU.mult).then_inc(hg_dve, 1)
                v.tensor_tensor(tq[:], tq[:], q[:], ALU.mult).then_inc(hg_dve, 1)
                v.wait_ge(hx_act, e0 + 9)
                v.tensor_tensor(Kx, Kx, Lg[:, d, :, 0, :], ALU.mult).then_inc(hg_dve, 1)
                order = (0, 1, 2, 3) if d == 0 else (3, 2, 1, 0)
                v.wait_ge(hg_pe, g0_ + 3)
                v.tensor_copy(St[:, order[0], :, :], px[0][:].rearrange("p (h e) -> p h e", h=HEADS)).then_inc(hg_dve, 1)
                for n in range(3):
                    v.wait_ge(hg_pe, g0_ + 6 + n)
                    if n:
                        S.sync()
                    v.wait_ge(hg_dve, 9 * d + 5 + n)
                    for h in range(HEADS):
                        c = h * CHUNKS + order[n]
                        a = v.scalar_tensor_tensor(out=St[:, order[n + 1], h, :], in0=St[:, order[n], h, :],
                                                   scalar=dec[:, c:c + 1], in1=px[n % 2][:, h * P:(h + 1) * P],
                                                   op0=ALU.mult, op1=ALU.add)
                        if h == HEADS - 1:
                            a.then_inc(hg_dve, 1)
                        else:
                            S.do(a)
                v.wait_ge(hg_pe, g0_ + 9)
                v.wait_ge(in_sgu, 48)
                mask = tri[:, d:d + 1, :].to_broadcast([P, HEADS, P])
                S.do(v.copy_predicated(sc[:, 0:HEADS, :], mask, px[0][:].rearrange("p (r t) -> p r t", t=P)))
                v.copy_predicated(sc[:, HEADS:, :], mask, px[1][:].rearrange("p (r t) -> p r t", t=P)) \
                 .then_inc(hg_dve, 1)

            def split(hi, lo, src):
                S.do(v.tensor_copy(hi, src))
                S.sync()
                v.tensor_tensor(lo, src, hi.bitcast(F32), ALU.subtract).then_inc(opnd, 1)

            def normalise_v():
                v.wait_ge(sg_pe, 1)
                S.do(v.tensor_scalar(lnv[:, 0, :], px[0][:, 0:T], 1.0 / (HEADS * P), None, ALU.mult))
                S.sync()
                S.do(tt_(lnv[:, 1, :], lnv[:, 0, :], lnv[:, 0, :], ALU.mult))
                v.wait_ge(sg_pe, 2)
                S.do(v.tensor_scalar(lnv[:, 2, :], px[1][:, 0:T], 1.0 / (HEADS * P), EPS, ALU.mult, ALU.add))
                S.sync()
                v.tensor_tensor(lnv[:, 3, :], lnv[:, 2, :], lnv[:, 1, :], ALU.subtract).then_inc(var_ready, 1)
                v.wait_ge(sd_ready, 8)
                S.do(v.reciprocal(lnv[:, 1, :], lnv[:, 3, :]))
                S.sync()

                def by_token(a):
                    return a.rearrange("p (n t) -> p n t", n=1).to_broadcast([P, HEADS, T])

                S.do(tt_(vn[:], v2[:], by_token(lnv[:, 0, :]), ALU.subtract))
                S.sync()
                S.do(tt_(vn[:], vn[:], by_token(lnv[:, 1, :]), ALU.mult))
                S.sync()
                for g in range(HEADS):
                    a = v.tensor_scalar(vn[:, g, :], vn[:, g, :], col("ln_v_g_2", g), col("ln_v_b_2", g), ALU.mult, ALU.add)
                    if g == HEADS - 1:
                        a.then_inc(sg_dve, 1)
                    else:
                        S.do(a)

            scans(0)
            scans(1)
            direction(0)
            direction(1)

            mods_used(18)
            S.do(tt_(gate2, mod[:, 6 * KT:7 * KT], col("b_mod_2", 2 * KT, KT), ALU.add))
            affine_cols(sc3, sh3, col("g_ffn_2", 0, KT), "b_mod_2", 3 * KT, 7 * KT)
            v.wait_ge(sg_pe, 5)
            for n in range(2):
                a = tt_(ob[:, 2 * n:2 * n + 2, :], px[n][:].rearrange("p (g t) -> p g t", g=2),
                        u2[:, 2 * n:2 * n + 2, :], ALU.mult)
                if n:
                    a.then_inc(sg_dve, 1)
                else:
                    S.do(a)
            S.sync()
            v.wait_ge(sg_dve, 2)
            split(ob_hi[:], ob_lo[:], ob[:])

            v.wait_ge(sg_pe, 6)
            S.do(v.tensor_scalar(ors[:, 0:2, :], px[0][:].rearrange("p (h t) -> p h t", h=2), 1.0 / P, EPS, ALU.mult,
                                 ALU.add))
            S.sync()
            v.wait_ge(sg_pe, 7)
            v.tensor_scalar(ors[:, 2:4, :], px[1][:].rearrange("p (h t) -> p h t", h=2), 1.0 / P, EPS, ALU.mult,
                            ALU.add).then_inc(var_ready, 1)
            v.wait_ge(sd_ready, 9)
            S.do(v.reciprocal(ors[:], ors[:]))
            S.sync()
            for n in range(2):
                S.do(tt_(o1[:, 2 * n:2 * n + 2, :], px[2 + n][:].rearrange("p (h t) -> p h t", h=2),
                         ors[:, 2 * n:2 * n + 2, :], ALU.mult))
            S.sync()
            for j in range(SLOTS):
                v.wait_ge(ps_free[j], BASE["uvo"] + 3)
            S.do(v.scalar_tensor_tensor(out=o1[:], in0=o1[:], scalar=col("g_norm_a_2"), in1=og2[:], op0=ALU.mult,
                                        op1=ALU.mult))
            S.sync()
            split(oa_hi[:], oa_lo[:], o1[:])

            for i in S.loop(ROUNDS_OF["pab"], 4):
                for e in range(2):
                    t = bass.ds(i * 4 + 2 * e, 2)
                    for part, gate in ((0, ga2), (1, gb2)):
                        j = 2 * e + part
                        v.wait_ge(pe_done[j], i + (BASE["pab"] + 1))
                        v.wait_ge(ps_free[j], i + BASE["pab"])
                        v.tensor_tensor(mt[:, e, part], ps[j][:].rearrange("p (n t) -> p n t", n=2), gate[:, t, :],
                                        ALU.mult).then_inc(ps_free[j], 1)
                    v.wait_ge(ps_free[2 * e], i + (BASE["pab"] + 1))
                    v.wait_ge(ps_free[2 * e + 1], i + (BASE["pab"] + 1))
                    S.do(tt_(mt[:, e, 0], mt[:, e, 0], mt[:, e, 1], ALU.add))
                    S.sync()
                    S.do(v.tensor_copy(m_hi[:, t, :], mt[:, e, 0]))
                    S.sync()
                    v.tensor_tensor(m_lo[:, t, :], mt[:, e, 0], m_hi[:, t, :].bitcast(F32), ALU.subtract) \
                     .then_inc(opnd, 1)
            add_to_x("wo", gate2)
            rstd(9, px[0][:, 0:T], D, EPS, v4[:, 0, :], v4[:, 1, :], 10)
            modulate(3 * KT, lambda k: x[:, k, :], v4[:, 1, :], sc3, sh3, t4, lambda k: h3_hi[:, k, :], lambda k: h3_lo[:, k, :])
            mod_tiles(18, 1)
            mod_tiles(19, 1)
            mods_used(20)
            S.do(tt_(gate3, mod[:, 9 * KT:10 * KT], col("b_mod_2", 5 * KT, KT), ALU.add))
            for i in S.loop(ROUNDS_OF["up"], 2):
                for e in range(2):
                    t = i * 2 + e
                    v.wait_ge(ps_free[2 * e], i + (BASE["up"] + 1))
                    v.wait_ge(pe_done[2 * e + 1], i + (BASE["up"] + 1))
                    v.wait_ge(ps_free[2 * e + 1], i + BASE["up"])
                    v.tensor_tensor(ff[:, e, :], ps[2 * e + 1][:, 0:T], sa[:, e, :], ALU.mult) \
                     .then_inc(ps_free[2 * e + 1], 1)
                    v.wait_ge(ps_free[2 * e + 1], i + (BASE["up"] + 1))
                    S.do(v.tensor_copy(ff_hi[:, t, :], ff[:, e, :]))
                    S.sync()
                    v.tensor_tensor(ff_lo[:, t, :], ff[:, e, :], ff_hi[:, t, :].bitcast(F32), ALU.subtract) \
                     .then_inc(opnd, 1)
            for name in ("dna", "dnb", "dnc"):
                add_to_x(name, gate3)
            rstd(10, px[0][:, 0:T], D, EPS, v4[:, 0, :], v4[:, 1, :], 11)
            for k in range(KT):
                v.scalar_tensor_tensor(out=x[:, k, :], in0=x[:, k, :], scalar=col("g_final_2", k), in1=v4[:, 1, :],
                                       op0=ALU.mult, op1=ALU.mult).then_inc(stored, 1)


def halves(w, tiles, k0=0, n=8):
    w = w[k0 * P:(k0 + n) * P]
    b = w.reshape(n, P, w.shape[1] // P, P)[:, :, list(tiles), :].transpose(2, 1, 0, 3)
    if n < 8:
        b = np.concatenate([b, np.zeros((b.shape[0], P, 8 - n, P), b.dtype)], axis=2)
    return b


def pairs(w):
    return w.reshape(4, P, w.shape[1] // (2 * P), 2, P).transpose(2, 1, 3, 0, 4).reshape(-1, P, 8, P)


def weight_stream(a):
    w = a["ev_w_in"][0]
    parts = [halves(w, range(24, 32))]
    va, vg = halves(w, range(0, 8)), halves(w, range(8, 16))
    parts.append(np.stack([va, vg], axis=1).reshape(16, P, 8, P))
    parts.append(halves(w, range(16, 24)))
    taps = np.zeros((CONV_TAPS + 1, KT // 2, P, P), w.dtype)
    taps[:CONV_TAPS, :, np.arange(P), np.arange(P)] = a["ev_conv_w"][0].reshape(CONV_TAPS, KT, P)[:, KT // 2:]
    cv = (taps.reshape(4, 8, KT // 2, P, P).transpose(0, 2, 3, 1, 4).reshape(16, P, 8, P))
    g = np.stack([a["ev_w_r"][0], a["ev_w_i"][0]], axis=1)
    g = g.transpose(2, 0, 1, 3, 4).reshape(4, 8, P, P).transpose(0, 2, 1, 3)
    gb = halves(w, range(32, 40))
    mixed = {name: np.empty((SLOTS, P, 8, P), w.dtype) for name in ("g0", "g1", "g2")}
    for blocks, slots in ((g, GATE_SLOT), (gb, GB_SLOT)):
        for block, (name, j) in zip(blocks, slots):
            mixed[name][j] = block
    parts += [mixed["g0"], cv, mixed["g1"], mixed["g2"]]
    w = a["ev_w_out"][0]
    parts += [halves(w, range(8), 0), halves(w, range(8), 8)]
    parts.append(halves(a["od_w_in"][0], range(32)))
    parts.append(np.concatenate([pairs(m) for m in a["od_w_grp"][0]]))
    w = a["od_w_out"][0]
    parts += [halves(w, range(8), 0), halves(w, range(8), 8)]
    w = a["w_in_2"][0]
    parts.append(halves(w, range(0, 16)))
    parts.append(halves(w, range(20, 28)))
    parts.append(halves(w, range(16, 20)))
    parts.append(halves(w, range(28, 44)))
    pab = np.stack([pairs(a["w_pa_2"][0]), pairs(a["w_pb_2"][0])], axis=1)
    parts.append(pab.reshape(8, P, 8, P))
    parts.append(halves(a["w_o_2"][0], range(8)))
    w = a["w_up_2"][0]
    up = np.stack([halves(w, range(FT)), halves(w, range(FT, 2 * FT))], axis=1)
    parts.append(up.reshape(2 * FT, P, 8, P))
    w = a["w_down_2"][0]
    parts += [halves(w, range(8), 0), halves(w, range(8), 8), halves(w, range(8), 16, 6)]
    return np.ascontiguousarray(np.concatenate(parts)).reshape(-1, P, 8, P)


def kernel(**inputs):
    import concourse.bacc as bacc
    from concourse.bass_utils import run_bass_kernel_spmd

    a = {n: np.asarray(v) for n, v in inputs.items()}

    def feature_major(v):
        return np.ascontiguousarray(v.reshape(T, KT, P).transpose(2, 1, 0))

    s, t = np.arange(P)[:, None], np.arange(P)[None, :]
    same = s // CHUNK == t // CHUNK
    tt = np.arange(T)
    count = []
    for w in WINDOWS:
        g = np.arange(GRID_W)
        count.append(np.minimum(g + w // 2, GRID_W) - np.maximum(g - w // 2, 0))
    rows = [np.eye(P), np.ones((P, T)), np.tile(tt % CHUNK != 0, (P, 1)), np.tile(tt % CHUNK != CHUNK - 1, (P, 1)),
            np.tile(1.0 / np.concatenate(count), (P, 1))]
    mod_w = np.concatenate([a["mod_w"][0][:, 2 * D:], a["mod_w"][1], a["w_mod_2"][0]], axis=1)
    arrays = {
        "c_cols": np.stack([a["c"][0], a["c_ctx"]], axis=1).reshape(KT, P, 2).transpose(1, 0, 2).reshape(P, 2 * KT),
        "c_rows": np.stack([a["c"][0], a["c_2"][0], a["c_ctx_2"]]),
        "mod0_w": a["mod_w"][0][:, :2 * D].reshape(KT, P, 2 * D),
        "mod_w": mod_w.T.reshape(MOD_TILES, P, D),
        "ctxT": feature_major(a["ctx"][0]),
        "xT": feature_major(a["x"][0]),
        "cols": np.concatenate([a[n].reshape(-1, P) for n, _ in PARAMS]).T,
        "con": np.concatenate([r.astype(np.float32) for r in rows], axis=1),
        "tri": np.stack([same & (s <= t), same & (s >= t)], axis=1).astype(np.int32),
        "ctx2T": feature_major(a["ctx_2"][0]),
        "wsT": a["w_s_2"][0].transpose(2, 0, 1),
        "b_s": a["b_s_2"].reshape(1, HEADS * P),
        "stream": weight_stream(a),
    }
    arrays = {n: np.ascontiguousarray(v) for n, v in arrays.items()}
    nc = bacc.Bacc("TRN2", target_bir_lowering=False, num_devices=1)
    ins = {n: nc.dram_tensor(f"in_{n}", v.shape, mybir.dt.from_np(v.dtype), kind="ExternalInput").ap()
           for n, v in arrays.items()}
    out = nc.dram_tensor("out_xT", (P, KT, T), F32, kind="ExternalOutput").ap()
    build(nc, ins, out)
    r = run_bass_kernel_spmd(nc, [{f"in_{n}": v for n, v in arrays.items()}], core_ids=[0])
    got = r.results[0]["out_xT"]
    return got.transpose(2, 1, 0).reshape(1, T, D)
```
